# Optimizing a Trainium2 kernel written in Bass

```python
import math
import jax, jax.numpy as jnp
from jax import lax
import numpy as np

D_MODEL = 2048
BATCH = 1
SEQ = 256
DEPTH = 1

GRID_W = 64
WIN_H = 8
WIN_W = 16
Q_BLOCK = 128
HEAD_DIM = 128
NA_WIDTH = D_MODEL // 2
NA_HEADS = NA_WIDTH // HEAD_DIM
SSM_WIDTH = D_MODEL // 4
SSM_CH = 16
SSM_GROUPS = SSM_WIDTH // SSM_CH
SSM_STATE = 64
MEM_WIDTH = D_MODEL // 4
MEM_HEADS = 4
MEM_HEAD_DIM = MEM_WIDTH // MEM_HEADS
N_MEM = 256
MIX_WIDTH = NA_WIDTH + SSM_WIDTH + MEM_WIDTH
IN_WIDTH = 3 * NA_WIDTH + SSM_WIDTH + MEM_WIDTH
D_FF = 4 * D_MODEL
EPS = 1e-6
DT_MIN = 1e-3
DT_MAX = 1e-1
LAM_RE_MAX = -1e-4


def rmsnorm(x, g):
    xf = x.astype(jnp.float32)
    y = xf * lax.rsqrt(jnp.mean(xf * xf, axis=-1, keepdims=True) + EPS)
    return (y * g.astype(jnp.float32)).astype(x.dtype)

def neighbourhood_tables(S):
    rows = S // GRID_W
    kh = min(WIN_H, rows)
    kw = min(WIN_W, GRID_W)
    t = jnp.arange(S, dtype=jnp.int32)
    r = t // GRID_W
    c = t % GRID_W
    rs = jnp.clip(r - kh // 2, 0, rows - kh)
    cs = jnp.clip(c - kw // 2, 0, GRID_W - kw)
    kr = rs[:, None, None] + jnp.arange(kh, dtype=jnp.int32)[None, :, None]
    kc = cs[:, None, None] + jnp.arange(kw, dtype=jnp.int32)[None, None, :]
    nbr = (kr * GRID_W + kc).reshape(S, kh * kw)
    off = ((kr - r[:, None, None] + WIN_H - 1) * (2 * WIN_W - 1)
           + (kc - c[:, None, None] + WIN_W - 1)).reshape(S, kh * kw)
    return nbr, off

def neighbourhood_attention(q, k, v, rpb):
    B, S, H, Dh = q.shape
    nbr, off = neighbourhood_tables(S)
    nk = nbr.shape[1]
    nb = S // Q_BLOCK
    rpb_flat = rpb.reshape(H, -1).astype(jnp.float32)
    scale = Dh ** -0.5
    qb = q.reshape(B, nb, Q_BLOCK, H, Dh).transpose(1, 0, 2, 3, 4)

    def block(args):
        q_blk, idx, bidx = args
        k_g = k[:, idx]
        v_g = v[:, idx]
        s = jnp.einsum('bqhd,bqkhd->bhqk', q_blk, k_g,
                       preferred_element_type=jnp.float32) * scale + rpb_flat[:, bidx][None]
        p = jax.nn.softmax(s, axis=-1).astype(v.dtype)
        return jnp.einsum('bhqk,bqkhd->bqhd', p, v_g)

    out = lax.map(block, (qb, nbr.reshape(nb, Q_BLOCK, nk), off.reshape(nb, Q_BLOCK, nk)))
    return out.transpose(1, 0, 2, 3, 4).reshape(B, S, H * Dh)

def s5_direction(u, lam_re, lam_im, log_dt, b_re, b_im, c_re, c_im, reverse):
    lam = lax.complex(jnp.minimum(lam_re.astype(jnp.float32), LAM_RE_MAX),
                      lam_im.astype(jnp.float32))
    dt = jnp.exp(log_dt.astype(jnp.float32))[:, None]
    lam_bar = jnp.exp(lam * dt)
    b = lax.complex(b_re.astype(jnp.float32), b_im.astype(jnp.float32))
    b_bar = ((lam_bar - 1.0) / lam)[..., None] * b
    bu = jnp.einsum('bsgc,gpc->bsgp', u.astype(jnp.complex64), b_bar)
    a = jnp.broadcast_to(lam_bar, bu.shape)

    def combine(e1, e2):
        a1, x1 = e1
        a2, x2 = e2
        return a1 * a2, a2 * x1 + x2

    _, h = lax.associative_scan(combine, (a, bu), axis=1, reverse=reverse)
    c = lax.complex(c_re.astype(jnp.float32), c_im.astype(jnp.float32))
    return jnp.einsum('bsgp,gcp->bsgc', h, c).real

def s5_mixer(u_flat, lam_re, lam_im, log_dt, b_re, b_im, c_re, c_im, d, w_glu, b_glu):
    B, S, _ = u_flat.shape
    u = u_flat.reshape(B, S, SSM_GROUPS, SSM_CH).astype(jnp.float32)
    y_f = s5_direction(u, lam_re[0], lam_im[0], log_dt[0], b_re[0], b_im[0], c_re[0], c_im[0], False)
    y_b = s5_direction(u, lam_re[1], lam_im[1], log_dt[1], b_re[1], b_im[1], c_re[1], c_im[1], True)
    y = (y_f + y_b + d.astype(jnp.float32) * u).reshape(B, S, SSM_WIDTH)
    y = jax.nn.gelu(y)
    y = y * jax.nn.sigmoid(y @ w_glu.astype(jnp.float32) + b_glu.astype(jnp.float32))
    return y.astype(u_flat.dtype)

def memory_cross_attention(q_flat, mem, mem_norm, w_mem_kv):
    B, S, _ = q_flat.shape
    q = q_flat.reshape(B, S, MEM_HEADS, MEM_HEAD_DIM)
    kv = rmsnorm(mem, mem_norm) @ w_mem_kv
    M = kv.shape[1]
    k, v = jnp.split(kv, 2, axis=-1)
    k = k.reshape(B, M, MEM_HEADS, MEM_HEAD_DIM)
    v = v.reshape(B, M, MEM_HEADS, MEM_HEAD_DIM)
    s = jnp.einsum('bshd,bmhd->bhsm', q, k, preferred_element_type=jnp.float32) * MEM_HEAD_DIM ** -0.5
    p = jax.nn.softmax(s, axis=-1).astype(v.dtype)
    return jnp.einsum('bhsm,bmhd->bshd', p, v).reshape(B, S, MEM_WIDTH)

def first_inputs(seed: int = 0) -> dict:
    key = jax.random.key(seed)
    ks = jax.random.split(key, 32)
    L = DEPTH
    f32 = jnp.float32

    def dense(k, shape, fan_in):
        return jax.random.normal(k, shape, f32) * fan_in ** -0.5

    def gain(k, shape):
        return 1.0 + 0.02 * jax.random.normal(k, shape, f32)

    n = jnp.arange(SSM_STATE, dtype=f32)
    G, P, Cg = SSM_GROUPS, SSM_STATE, SSM_CH
    return {
        "x": jax.random.normal(ks[0], (BATCH, SEQ, D_MODEL), f32),
        "mem": jax.random.normal(ks[1], (BATCH, N_MEM, D_MODEL), f32),
        "norm_mix_pre": gain(ks[2], (L, D_MODEL)),
        "w_in": dense(ks[3], (L, D_MODEL, IN_WIDTH), D_MODEL),
        "na_rpb": 0.02 * jax.random.normal(ks[4], (L, NA_HEADS, 2 * WIN_H - 1, 2 * WIN_W - 1), f32),
        "ssm_lam_re": -0.5 + 0.01 * jax.random.normal(ks[5], (L, 2, G, P), f32),
        "ssm_lam_im": math.pi * n + 0.01 * jax.random.normal(ks[6], (L, 2, G, P), f32),
        "ssm_log_dt": jax.random.uniform(ks[7], (L, 2, G), f32, math.log(DT_MIN), math.log(DT_MAX)),
        "ssm_b_re": dense(ks[8], (L, 2, G, P, Cg), 2 * Cg),
        "ssm_b_im": dense(ks[9], (L, 2, G, P, Cg), 2 * Cg),
        "ssm_c_re": dense(ks[10], (L, 2, G, Cg, P), 2 * P),
        "ssm_c_im": dense(ks[11], (L, 2, G, Cg, P), 2 * P),
        "ssm_d": jax.random.normal(ks[12], (L, G, Cg), f32),
        "w_glu": dense(ks[13], (L, SSM_WIDTH, SSM_WIDTH), SSM_WIDTH),
        "b_glu": 0.01 * jax.random.normal(ks[14], (L, SSM_WIDTH), f32),
        "mem_norm": gain(ks[15], (L, D_MODEL)),
        "w_mem_kv": dense(ks[16], (L, D_MODEL, 2 * MEM_WIDTH), D_MODEL),
        "out_norm_na": gain(ks[17], (L, NA_WIDTH)),
        "out_norm_ssm": gain(ks[18], (L, SSM_WIDTH)),
        "out_norm_mem": gain(ks[19], (L, MEM_WIDTH)),
        "w_out": dense(ks[20], (L, MIX_WIDTH, D_MODEL), MIX_WIDTH),
        "norm_mix_post": gain(ks[21], (L, D_MODEL)),
        "norm_mlp_pre": gain(ks[22], (L, D_MODEL)),
        "w_ff1": dense(ks[23], (L, D_MODEL, D_FF), D_MODEL),
        "w_ff2": dense(ks[24], (L, D_FF, D_MODEL), D_FF),
        "norm_mlp_post": gain(ks[25], (L, D_MODEL)),
    }

def first_block(x, mem, norm_mix_pre, w_in, na_rpb, ssm_lam_re, ssm_lam_im, ssm_log_dt,
              ssm_b_re, ssm_b_im, ssm_c_re, ssm_c_im, ssm_d, w_glu, b_glu, mem_norm,
              w_mem_kv, out_norm_na, out_norm_ssm, out_norm_mem, w_out, norm_mix_post,
              norm_mlp_pre, w_ff1, w_ff2, norm_mlp_post):
    B, S, _ = x.shape
    for l in range(DEPTH):
        h = rmsnorm(x, norm_mix_pre[l])
        proj = h @ w_in[l]
        q_na, k_na, v_na, u_ssm, q_mem = jnp.split(
            proj, [NA_WIDTH, 2 * NA_WIDTH, 3 * NA_WIDTH, 3 * NA_WIDTH + SSM_WIDTH], axis=-1)
        hs = (B, S, NA_HEADS, HEAD_DIM)
        y_na = neighbourhood_attention(q_na.reshape(hs), k_na.reshape(hs), v_na.reshape(hs), na_rpb[l])
        y_ssm = s5_mixer(u_ssm, ssm_lam_re[l], ssm_lam_im[l], ssm_log_dt[l], ssm_b_re[l], ssm_b_im[l],
                         ssm_c_re[l], ssm_c_im[l], ssm_d[l], w_glu[l], b_glu[l])
        y_mem = memory_cross_attention(q_mem, mem, mem_norm[l], w_mem_kv[l])
        y = jnp.concatenate([rmsnorm(y_na, out_norm_na[l]),
                             rmsnorm(y_ssm, out_norm_ssm[l]),
                             rmsnorm(y_mem, out_norm_mem[l])], axis=-1)
        x = x + rmsnorm(y @ w_out[l], norm_mix_post[l])
        h = rmsnorm(x, norm_mlp_pre[l])
        f = jnp.square(jax.nn.relu(h @ w_ff1[l])) @ w_ff2[l]
        x = x + rmsnorm(f, norm_mlp_post[l])
    return x


_first_inputs = first_inputs


def first_inputs(seed=0):
    import zlib

    import numpy as np

    out = dict(_first_inputs(seed))
    spreads = {}
    factors = {}
    for name, (base, spread) in spreads.items():
        noise = np.random.default_rng([zlib.crc32(name.encode()), seed]).standard_normal(out[name].shape)
        drawn = base * np.exp(spread * noise) if base else spread * noise
        out[name] = __import__('jax').numpy.asarray(drawn.astype(out[name].dtype))
    for name, factor in factors.items():
        out[name] = (out[name] * factor).astype(out[name].dtype)
    return out


_narrow_inputs = first_inputs


def first_inputs(seed=0):

    out = dict(_narrow_inputs(seed))
    wider = {'norm_mix_pre': 3.01,
     'na_rpb': 6.47,
     'ssm_lam_re': 12.0,
     'b_glu': 12.0,
     'mem_norm': 5.88,
     'out_norm_na': 6.17,
     'out_norm_ssm': 8.79,
     'out_norm_mem': 9.28,
     'norm_mix_post': 4.21,
     'norm_mlp_pre': 4.79,
     'norm_mlp_post': 5.35}
    for name, times in wider.items():
        mean = out[name].mean()
        out[name] = (mean + times * (out[name] - mean)).astype(out[name].dtype)
    return out


HEAD_DIM_2 = 64
GROUP_HEADS = 8
GROUP_WIDTH = GROUP_HEADS * HEAD_DIM_2
N_GROUPS = 4
MIX_WIDTH_2 = N_GROUPS * GROUP_WIDTH
D_FF_2 = 4 * D_MODEL
NEG_INF = -1e30
BIG = 1e9

MLA_Q_RANK = 384
MLA_KV_RANK = 128
MLA_NOPE = 64
MLA_ROPE = 32
MLA_V = HEAD_DIM_2
ROPE_THETA = 10000.0

NSA_KV_HEADS = 2
NSA_KV_WIDTH = NSA_KV_HEADS * HEAD_DIM_2
NSA_CMP_LEN = 32
NSA_CMP_STRIDE = 16
NSA_SEL_LEN = 64
NSA_TOP_N = 8
NSA_WINDOW = 256

SWA_KV_HEADS = 2
SWA_KV_WIDTH = SWA_KV_HEADS * HEAD_DIM_2
SWA_WINDOW = 128

REL_BUCKETS = 32
REL_MAX_DIST = 128
REL_HEADS = 2 * GROUP_HEADS

IN_SPLITS = (
    MLA_Q_RANK, MLA_KV_RANK, MLA_ROPE,
    GROUP_WIDTH, GROUP_WIDTH, GROUP_WIDTH, GROUP_HEADS,
    GROUP_WIDTH, NSA_KV_WIDTH, NSA_KV_WIDTH, NSA_KV_WIDTH,
    NSA_KV_WIDTH, NSA_KV_WIDTH, NSA_KV_WIDTH, 3 * GROUP_HEADS,
    GROUP_WIDTH, SWA_KV_WIDTH, SWA_KV_WIDTH,
)
IN_COLS = sum(IN_SPLITS)


def rmsnorm_2(x, g):
    xf = x.astype(jnp.float32)
    y = xf * lax.rsqrt(jnp.mean(xf * xf, axis=-1, keepdims=True) + EPS)
    return (y * g.astype(jnp.float32)).astype(x.dtype)

def split_heads(x, h):
    b, t, _ = x.shape
    return x.reshape(b, t, h, -1).transpose(0, 2, 1, 3)

def merge_heads(x):
    b, h, t, d = x.shape
    return x.transpose(0, 2, 1, 3).reshape(b, t, h * d)

def rope(x, pos):
    d = x.shape[-1]
    inv = ROPE_THETA ** (-jnp.arange(0, d, 2, dtype=jnp.float32) / d)
    ang = pos.astype(jnp.float32)[:, None] * inv[None, :]
    cos, sin = jnp.cos(ang), jnp.sin(ang)
    x1 = x[..., : d // 2].astype(jnp.float32)
    x2 = x[..., d // 2:].astype(jnp.float32)
    return jnp.concatenate([x1 * cos - x2 * sin, x1 * sin + x2 * cos], axis=-1).astype(x.dtype)

def t5_bucket(dist):
    max_exact = REL_BUCKETS // 2
    d = jnp.maximum(dist, 0)
    large = max_exact + (jnp.log(jnp.maximum(d, 1).astype(jnp.float32) / max_exact)
                         / math.log(REL_MAX_DIST / max_exact)
                         * (REL_BUCKETS - max_exact)).astype(jnp.int32)
    large = jnp.minimum(large, REL_BUCKETS - 1)
    return jnp.where(d < max_exact, d, large)

def dense_causal_attention(q, k, v, scale, fcum=None):
    b, h, t, dk = q.shape
    nb = t // Q_BLOCK
    kpos = jnp.arange(t)
    qb = q.reshape(b, h, nb, Q_BLOCK, dk).transpose(2, 0, 1, 3, 4)
    xs = (jnp.arange(nb), qb)
    if fcum is not None:
        xs = xs + (fcum.reshape(b, h, nb, Q_BLOCK).transpose(2, 0, 1, 3),)

    def one_block(args):
        i, qi = args[0], args[1]
        s = jnp.einsum('bhqd,bhkd->bhqk', qi, k, preferred_element_type=jnp.float32) * scale
        if fcum is not None:
            s = s + args[2][..., :, None] - fcum[:, :, None, :]
        qpos = i * Q_BLOCK + jnp.arange(Q_BLOCK)
        s = jnp.where(kpos[None, :] <= qpos[:, None], s, NEG_INF)
        p = jax.nn.softmax(s, axis=-1)
        return jnp.einsum('bhqk,bhkd->bhqd', p.astype(v.dtype), v)

    o = lax.map(one_block, xs)
    return o.transpose(1, 2, 0, 3, 4).reshape(b, h, t, v.shape[-1])

def banded_attention(q, k, v, window, tbl, sinks=None):
    b, g, r, t, d = q.shape
    nb, nw = t // Q_BLOCK, window // Q_BLOCK

    def blocks(a):
        ap = jnp.pad(a, ((0, 0), (0, 0), (window, 0), (0, 0))).reshape(b, g, nb + nw, Q_BLOCK, d)
        return jnp.concatenate([ap[:, :, i:i + nb] for i in range(nw + 1)], axis=3)

    kb, vb = blocks(k), blocks(v)
    qb = q.reshape(b, g, r, nb, Q_BLOCK, d)
    s = jnp.einsum('bgrnqd,bgnkd->bgrnqk', qb, kb, preferred_element_type=jnp.float32) * d ** -0.5
    kw = (nw + 1) * Q_BLOCK
    dist = (jnp.arange(Q_BLOCK)[:, None] + window) - jnp.arange(kw)[None, :]
    key_real = jnp.arange(nb)[:, None, None] * Q_BLOCK - window + jnp.arange(kw)[None, None, :]
    mask = (dist >= 0) & (dist < window) & (key_real >= 0)
    s = s + tbl[:, :, t5_bucket(dist)][:, :, None].astype(jnp.float32)
    s = jnp.where(mask, s, NEG_INF)
    if sinks is not None:
        sink = jnp.broadcast_to(sinks.astype(jnp.float32)[None, :, :, None, None, None], s.shape[:-1] + (1,))
        p = jax.nn.softmax(jnp.concatenate([s, sink], axis=-1), axis=-1)[..., :-1]
    else:
        p = jax.nn.softmax(s, axis=-1)
    o = jnp.einsum('bgrnqk,bgnkd->bgrnqd', p.astype(v.dtype), vb)
    return o.reshape(b, g, r, t, d)

def mla_mixer(c_q, c_kv, k_pe, q_norm, w_uq, kv_norm, w_ukv, pos):
    b, t, _ = c_q.shape
    q = split_heads(rmsnorm_2(c_q, q_norm) @ w_uq, GROUP_HEADS)
    q = jnp.concatenate([q[..., :MLA_NOPE], rope(q[..., MLA_NOPE:], pos)], axis=-1)
    kv = split_heads(rmsnorm_2(c_kv, kv_norm) @ w_ukv, GROUP_HEADS)
    k_pe = jnp.broadcast_to(rope(k_pe[:, None], pos), (b, GROUP_HEADS, t, MLA_ROPE))
    k = jnp.concatenate([kv[..., :MLA_NOPE], k_pe], axis=-1)
    v = kv[..., MLA_NOPE:]
    o = dense_causal_attention(q, k, v, (MLA_NOPE + MLA_ROPE) ** -0.5)
    return merge_heads(o)

def fox_mixer(q, k, v, f_logit, b_f):
    log_f = jax.nn.log_sigmoid(f_logit.astype(jnp.float32) + b_f.astype(jnp.float32))
    fcum = jnp.cumsum(log_f, axis=1).transpose(0, 2, 1)
    o = dense_causal_attention(split_heads(q, GROUP_HEADS), split_heads(k, GROUP_HEADS),
                               split_heads(v, GROUP_HEADS), HEAD_DIM_2 ** -0.5, fcum)
    return merge_heads(o)

def nsa_compress(kv, pos_emb, w1, w2):
    b, g, t, d = kv.shape
    nc = (t - NSA_CMP_LEN) // NSA_CMP_STRIDE + 1
    idx = jnp.arange(nc)[:, None] * NSA_CMP_STRIDE + jnp.arange(NSA_CMP_LEN)[None, :]
    blk = kv[:, :, idx] + pos_emb
    flat = blk.reshape(b, g, nc, NSA_CMP_LEN * d)
    return jax.nn.gelu(flat @ w1) @ w2

def nsa_cmp_sel(qg, k_cmp, v_cmp, ks, vs, tbl):
    b, g, r, t, d = qg.shape
    nb = t // Q_BLOCK
    nc = k_cmp.shape[2]
    ns = t // NSA_SEL_LEN
    n_top = min(NSA_TOP_N, ns)
    scale = d ** -0.5
    cmp_end = jnp.arange(nc) * NSA_CMP_STRIDE + NSA_CMP_LEN - 1
    ci = jnp.arange(nc)[:, None]
    sj = jnp.arange(ns)[None, :]
    overlap = ((ci * NSA_CMP_STRIDE + NSA_CMP_LEN - 1 >= sj * NSA_SEL_LEN)
               & (ci * NSA_CMP_STRIDE <= sj * NSA_SEL_LEN + NSA_SEL_LEN - 1)).astype(jnp.float32)
    ks_blk = ks.reshape(b, g, ns, NSA_SEL_LEN, d)
    vs_blk = vs.reshape(b, g, ns, NSA_SEL_LEN, d)
    bi = jnp.arange(b)[:, None, None, None]
    gi = jnp.arange(g)[None, :, None, None]
    g_ix = jnp.arange(g)[None, :, None, None, None]
    r_ix = jnp.arange(r)[None, None, :, None, None]
    jsel = jnp.arange(ns)
    qb = qg.reshape(b, g, r, nb, Q_BLOCK, d).transpose(3, 0, 1, 2, 4, 5)

    def one_block(args):
        n, qi = args
        qpos = n * Q_BLOCK + jnp.arange(Q_BLOCK)
        sc = jnp.einsum('bgrqd,bgcd->bgrqc', qi, k_cmp, preferred_element_type=jnp.float32) * scale
        dist_c = qpos[:, None] - cmp_end[None, :]
        valid_c = dist_c >= 0
        sc = sc + tbl[:, :, t5_bucket(dist_c)].astype(jnp.float32)
        sc = jnp.where(valid_c, sc, NEG_INF)
        pc = jnp.where(valid_c, jax.nn.softmax(sc, axis=-1), 0.0)
        o_cmp = jnp.einsum('bgrqc,bgcd->bgrqd', pc.astype(v_cmp.dtype), v_cmp)
        imp = jnp.einsum('bgrqc,cs->bgqs', pc, overlap)
        cur = (qpos // NSA_SEL_LEN)[:, None]
        forced = (jsel[None, :] == 0) | (jsel[None, :] == cur) | (jsel[None, :] == cur - 1)
        score = jnp.where(jsel[None, :] <= cur, jnp.where(forced, BIG, imp), NEG_INF)
        _, sel = lax.top_k(score, n_top)
        k_sel = ks_blk[bi, gi, sel].reshape(b, g, Q_BLOCK, n_top * NSA_SEL_LEN, d)
        v_sel = vs_blk[bi, gi, sel].reshape(b, g, Q_BLOCK, n_top * NSA_SEL_LEN, d)
        kpos = (sel[..., None] * NSA_SEL_LEN + jnp.arange(NSA_SEL_LEN)).reshape(b, g, Q_BLOCK, n_top * NSA_SEL_LEN)
        dist_s = qpos[None, None, :, None] - kpos
        ss = jnp.einsum('bgrqd,bgqkd->bgrqk', qi, k_sel, preferred_element_type=jnp.float32) * scale
        ss = ss + tbl[g_ix, r_ix, t5_bucket(dist_s)[:, :, None]].astype(jnp.float32)
        ss = jnp.where(dist_s[:, :, None] >= 0, ss, NEG_INF)
        ps = jax.nn.softmax(ss, axis=-1)
        o_sel = jnp.einsum('bgrqk,bgqkd->bgrqd', ps.astype(v_sel.dtype), v_sel)
        return o_cmp, o_sel

    o_cmp, o_sel = lax.map(one_block, (jnp.arange(nb), qb))
    fix = lambda o: o.transpose(1, 2, 3, 0, 4, 5).reshape(b, g, r, t, d)
    return fix(o_cmp), fix(o_sel)

def nsa_mixer(q, kc, vc, ksl, vsl, kwn, vwn, gate, cmp_pos, cmp_w1, cmp_w2, tbl):
    b, t, _ = q.shape
    g, r = NSA_KV_HEADS, GROUP_HEADS // NSA_KV_HEADS
    qg = split_heads(q, GROUP_HEADS).reshape(b, g, r, t, HEAD_DIM_2)
    kc, vc = split_heads(kc, g), split_heads(vc, g)
    ksl, vsl = split_heads(ksl, g), split_heads(vsl, g)
    kwn, vwn = split_heads(kwn, g), split_heads(vwn, g)
    k_cmp = nsa_compress(kc, cmp_pos[0], cmp_w1[0], cmp_w2[0])
    v_cmp = nsa_compress(vc, cmp_pos[1], cmp_w1[1], cmp_w2[1])
    o_cmp, o_sel = nsa_cmp_sel(qg, k_cmp, v_cmp, ksl, vsl, tbl)
    o_win = banded_attention(qg, kwn, vwn, NSA_WINDOW, tbl)
    gts = jax.nn.sigmoid(gate).reshape(b, t, g, r, 3).transpose(0, 2, 3, 1, 4)
    o = gts[..., 0:1] * o_cmp + gts[..., 1:2] * o_sel + gts[..., 2:3] * o_win
    return merge_heads(o.reshape(b, GROUP_HEADS, t, HEAD_DIM_2))

def swa_mixer(q, k, v, sinks, tbl):
    b, t, _ = q.shape
    g, r = SWA_KV_HEADS, GROUP_HEADS // SWA_KV_HEADS
    qg = split_heads(q, GROUP_HEADS).reshape(b, g, r, t, HEAD_DIM_2)
    o = banded_attention(qg, split_heads(k, g), split_heads(v, g), SWA_WINDOW, tbl, sinks.reshape(g, r))
    return merge_heads(o.reshape(b, GROUP_HEADS, t, HEAD_DIM_2))

def second_inputs(seed: int = 0) -> dict:
    key = jax.random.key(seed)
    ks = jax.random.split(key, 20)
    nrm = lambda k, shape, fan_in: jax.random.normal(k, shape, jnp.float32) * fan_in ** -0.5
    gain = lambda k, shape: 1.0 + 0.05 * jax.random.normal(k, shape, jnp.float32)
    L = DEPTH
    return {
        'x': jax.random.normal(ks[0], (BATCH, SEQ, D_MODEL), jnp.float32),
        'norm_attn': gain(ks[1], (L, D_MODEL)),
        'w_in': nrm(ks[2], (L, D_MODEL, IN_COLS), D_MODEL),
        'mla_q_norm': gain(ks[3], (L, MLA_Q_RANK)),
        'mla_w_uq': nrm(ks[4], (L, MLA_Q_RANK, GROUP_HEADS * (MLA_NOPE + MLA_ROPE)), MLA_Q_RANK),
        'mla_kv_norm': gain(ks[5], (L, MLA_KV_RANK)),
        'mla_w_ukv': nrm(ks[6], (L, MLA_KV_RANK, GROUP_HEADS * (MLA_NOPE + MLA_V)), MLA_KV_RANK),
        'fox_b_f': 3.0 + 0.5 * jax.random.normal(ks[7], (L, GROUP_HEADS), jnp.float32),
        'nsa_cmp_pos': 0.1 * jax.random.normal(ks[8], (L, 2, NSA_CMP_LEN, HEAD_DIM_2), jnp.float32),
        'nsa_cmp_w1': nrm(ks[9], (L, 2, NSA_CMP_LEN * HEAD_DIM_2, HEAD_DIM_2), NSA_CMP_LEN * HEAD_DIM_2),
        'nsa_cmp_w2': nrm(ks[10], (L, 2, HEAD_DIM_2, HEAD_DIM_2), HEAD_DIM_2),
        'swa_sinks': 0.5 * jax.random.normal(ks[11], (L, GROUP_HEADS), jnp.float32),
        'group_norm': gain(ks[12], (L, MIX_WIDTH_2)),
        'w_out': nrm(ks[13], (L, MIX_WIDTH_2, D_MODEL), MIX_WIDTH_2),
        'norm_mlp': gain(ks[14], (L, D_MODEL)),
        'w_up': nrm(ks[15], (L, D_MODEL, D_FF_2), D_MODEL),
        'w_down': nrm(ks[16], (L, D_FF_2, D_MODEL), D_FF_2),
        'rel_bias': 0.5 * jax.random.normal(ks[17], (REL_BUCKETS, REL_HEADS), jnp.float32),
        'final_norm': gain(ks[18], (D_MODEL,)),
    }

def second_block(x, norm_attn, w_in, mla_q_norm, mla_w_uq, mla_kv_norm, mla_w_ukv, fox_b_f,
              nsa_cmp_pos, nsa_cmp_w1, nsa_cmp_w2, swa_sinks, group_norm, w_out,
              norm_mlp, w_up, w_down, rel_bias, final_norm):
    b, t, _ = x.shape
    pos = jnp.arange(t)
    r_nsa = GROUP_HEADS // NSA_KV_HEADS
    r_swa = GROUP_HEADS // SWA_KV_HEADS
    tbl_nsa = rel_bias[:, :GROUP_HEADS].T.reshape(NSA_KV_HEADS, r_nsa, REL_BUCKETS)
    tbl_swa = rel_bias[:, GROUP_HEADS:].T.reshape(SWA_KV_HEADS, r_swa, REL_BUCKETS)
    offsets = [int(o) for o in np.cumsum(IN_SPLITS)[:-1]]
    h = x
    for l in range(DEPTH):
        u = rmsnorm_2(h, norm_attn[l])
        p = jnp.split(u @ w_in[l], offsets, axis=-1)
        o_mla = mla_mixer(p[0], p[1], p[2], mla_q_norm[l], mla_w_uq[l], mla_kv_norm[l], mla_w_ukv[l], pos)
        o_fox = fox_mixer(p[3], p[4], p[5], p[6], fox_b_f[l])
        o_nsa = nsa_mixer(p[7], p[8], p[9], p[10], p[11], p[12], p[13], p[14],
                          nsa_cmp_pos[l], nsa_cmp_w1[l], nsa_cmp_w2[l], tbl_nsa)
        o_swa = swa_mixer(p[15], p[16], p[17], swa_sinks[l], tbl_swa)
        o = jnp.concatenate([o_mla, o_fox, o_nsa, o_swa], axis=-1).reshape(b, t, N_GROUPS, GROUP_WIDTH)
        o = rmsnorm_2(o, group_norm[l].reshape(N_GROUPS, GROUP_WIDTH)).reshape(b, t, MIX_WIDTH_2)
        h = h + o @ w_out[l]
        m = rmsnorm_2(h, norm_mlp[l]) @ w_up[l]
        h = h + jnp.square(jax.nn.relu(m)) @ w_down[l]
    return rmsnorm_2(h, final_norm)


def setup_inputs(seed=0):
    out = dict(first_inputs(seed))
    for name, value in second_inputs(seed + 1).items():
        if name != "x":
            out[name + "_2"] = value
    return out


def reference(
    x, mem, norm_mix_pre, w_in, na_rpb, ssm_lam_re, ssm_lam_im, ssm_log_dt, ssm_b_re, ssm_b_im,
    ssm_c_re, ssm_c_im, ssm_d, w_glu, b_glu, mem_norm, w_mem_kv, out_norm_na, out_norm_ssm,
    out_norm_mem, w_out, norm_mix_post, norm_mlp_pre, w_ff1, w_ff2, norm_mlp_post, norm_attn_2,
    w_in_2, mla_q_norm_2, mla_w_uq_2, mla_kv_norm_2, mla_w_ukv_2, fox_b_f_2, nsa_cmp_pos_2,
    nsa_cmp_w1_2, nsa_cmp_w2_2, swa_sinks_2, group_norm_2, w_out_2, norm_mlp_2, w_up_2,
    w_down_2, rel_bias_2, final_norm_2,
):
    x = first_block(
        x, mem, norm_mix_pre, w_in, na_rpb, ssm_lam_re, ssm_lam_im, ssm_log_dt, ssm_b_re,
        ssm_b_im, ssm_c_re, ssm_c_im, ssm_d, w_glu, b_glu, mem_norm, w_mem_kv, out_norm_na,
        out_norm_ssm, out_norm_mem, w_out, norm_mix_post, norm_mlp_pre, w_ff1, w_ff2,
        norm_mlp_post,
    )
    return second_block(
        x, norm_attn_2, w_in_2, mla_q_norm_2, mla_w_uq_2, mla_kv_norm_2, mla_w_ukv_2, fox_b_f_2,
        nsa_cmp_pos_2, nsa_cmp_w1_2, nsa_cmp_w2_2, swa_sinks_2, group_norm_2, w_out_2,
        norm_mlp_2, w_up_2, w_down_2, rel_bias_2, final_norm_2,
    )


_drawn_inputs = setup_inputs


def setup_inputs(seed=0):
    import zlib

    import numpy as np

    out = dict(_drawn_inputs(seed))
    spreads = {}
    factors = {'ssm_lam_re': 64.0,
     'b_glu': 3.181,
     'mla_q_norm_2': 8.0,
     'mla_kv_norm_2': 3.906,
     'fox_b_f_2': 23.344,
     'nsa_cmp_pos_2': 3.379,
     'swa_sinks_2': 8.0,
     'ssm_b_re': 3.49,
     'ssm_b_im': 3.377,
     'ssm_c_re': 3.415,
     'ssm_c_im': 3.537}
    for name, (base, spread) in spreads.items():
        noise = np.random.default_rng([zlib.crc32(name.encode()), seed]).standard_normal(out[name].shape)
        drawn = base * np.exp(spread * noise) if base else spread * noise
        out[name] = __import__('jax').numpy.asarray(drawn.astype(out[name].dtype))
    for name, factor in factors.items():
        out[name] = (out[name] * factor).astype(out[name].dtype)
    return out
```

```python
import concourse.bass as bass
from concourse import mybir
from contextlib import ExitStack
import numpy as np

S = 256
P = 128
TT = S // P
D = 2048
KT = D // P
DFF = 4 * D
FT = DFF // P
EPS = 1e-6
NEG = -1e30

GRID_W, WIN_H, WIN_W = 64, 8, 16
RPB_W = 2 * WIN_W - 1
RPB_H = 2 * WIN_H - 1
NA_HEADS, NA_D = 8, 128
MEM_HEADS, MEM_D = 4, 128
GROUPS, CH, ST = 32, 16, 64
SSM_W = 512
CHUNKS = 8
LAM_MAX = -1e-4

HEADS, HD = 8, 64
ROPE = 32
NOPE = 64
CMP_LEN, CMP_STRIDE = 32, 16
NCMP = (S - CMP_LEN) // CMP_STRIDE + 1
BUCKETS, MAX_DIST = 32, 128
SWA_WIN = 128

RING = 8
SLOT = 2048
SK = SLOT // 512

GAINS = [("mix_pre", 16), ("mem", 16), ("out", 16), ("post", 16), ("mlp_pre", 16), ("mlp_post", 16),
         ("b_glu", 4), ("ssm_d", 4), ("attn2", 16), ("mla_q", 3), ("mla_kv", 1), ("group", 16),
         ("mlp2", 16), ("final", 16), ("b_f", 1), ("sinks", 8)]
GCOL = {}
for _n, _w in GAINS:
    GCOL[_n] = sum(w for n, w in GAINS if n in GCOL)
NG = sum(w for _, w in GAINS)

W1_GROUPS = ["memk", "memv", "u", "q0", "q1", "k0", "k1", "v0", "v1", "qm"]
W2_GROUPS = ["mla_c", "fq", "fk", "fv", "nq", "nk", "nv", "sq", "small"]


def ring_plan():
    n, at = 0, {}
    for name, slots in ([(g, 4) for g in W1_GROUPS] + [("glu", 1), ("wout1", 16), ("ff1_1", 64), ("ff2_1", 64)]
                        + [(g, 4) for g in W2_GROUPS[:-1]] + [("small", 2), ("cmpk", 1), ("cmpv", 1), ("uqa", 1), ("uqb", 1), ("ukv", 1)]
                        + [("wout2", 16), ("ff1_2", 64), ("ff2_2", 64)]):
        at[name] = n
        n += slots
    return at


def acc_plan():
    n, at = 0, {}
    for name, k in ([(g, 1) for g in W1_GROUPS] + [("glu", 1), ("wout1", 4), ("ff1_1", 16), ("ff2_1", 4)]
                    + [(g, 1) for g in W2_GROUPS] + [("cmpk", 1), ("cmpk2", 1), ("cmpv", 1), ("cmpv2", 1), ("uqa", 1), ("uqar", 1), ("uqb", 1), ("uqbr", 1), ("kper", 1), ("kna", 1), ("knb", 1), ("mv", 1)]
                    + [("wout2", 4), ("ff1_2", 16), ("ff2_2", 4)]):
        at[name] = n
        n += k
    return at


SLOT0 = ring_plan()
ACC0 = acc_plan()


def t5_bucket(d):
    exact = BUCKETS // 2
    d = np.maximum(d, 0)
    large = exact + (np.log(np.maximum(d, 1).astype(np.float32) / np.float32(exact))
                     / np.float32(np.log(MAX_DIST / exact)) * np.float32(BUCKETS - exact)).astype(np.int32)
    return np.where(d < exact, d, np.minimum(large, BUCKETS - 1))


def constants():
    f = np.float32
    c = {}
    c["ident"] = np.eye(P, dtype=f)
    c["iota"] = np.tile(np.arange(S, dtype=f), (P, 1))
    q = np.arange(S)
    cq, cs = q % GRID_W, np.clip(q % GRID_W - WIN_W // 2, 0, GRID_W - WIN_W)
    inside = (cq[None] >= cs[:, None]) & (cq[None] < cs[:, None] + WIN_W)
    tile = lambda m: np.ascontiguousarray(m.reshape(TT, P, -1).transpose(1, 0, 2).reshape(P, -1))
    c["na_mask"] = tile(np.where(inside, 0, NEG).astype(f))
    causal = tile(np.where(q[None] <= q[:, None], 0, NEG).astype(f))
    ends = np.arange(NCMP) * CMP_STRIDE + CMP_LEN - 1
    valid = np.zeros((P, 32), f)
    valid[:, :TT * NCMP] = tile((q[:, None] >= ends[None]).astype(f))
    inv = (f(10000.0) ** (-np.arange(0, ROPE, 2, dtype=f) / f(ROPE))).astype(f)
    ang = q.astype(f)[None] * inv[:, None]
    cos, sin = np.ones((P, S), f), np.zeros((P, S), f)
    cos[NOPE:NOPE + 16] = cos[NOPE + 16:NOPE + 32] = np.cos(ang)
    sin[NOPE:NOPE + 16] = sin[NOPE + 16:NOPE + 32] = np.sin(ang)
    turn = np.zeros((P, NOPE + ROPE), f)
    for j in range(16):
        turn[NOPE + 16 + j, NOPE + j] = -1
        turn[NOPE + j, NOPE + 16 + j] = 1
    c["block2"] = np.concatenate([causal, valid, cos, sin, turn], 1)
    j = np.arange(2 * S)
    dist = S - 1 - j
    hot = np.zeros((P, 2 * S), f)
    hot[t5_bucket(dist), j] = 1
    mask = np.zeros((P, 2 * S), f)
    mask[:2 * HEADS, dist < 0] = NEG
    mask[HEADS:2 * HEADS, dist >= SWA_WIN] = NEG
    c["t5"] = np.concatenate([hot, mask], 1)
    return c


class Marks:

    def __init__(self, eng, sem, book):
        self.eng, self.sem, self.book, self.n = eng, sem, book, 0

    def did(self, ins, *name):
        ins.then_inc(self.sem, 1)
        self.n += 1
        if name:
            self.book[name] = self.n

    def own(self):
        self.eng.wait_ge(self.sem, self.n)


def program(nc, A, out, seen, book):
    f32 = mybir.dt.float32
    ALU = mybir.AluOpType
    ACT = mybir.ActivationFunctionType
    AX = mybir.AxisListType
    ctx = ExitStack()
    with ctx:
        def sb(name, cols):
            return ctx.enter_context(nc.sbuf_tensor(name, [P, cols], f32))

        def sem(name):
            return ctx.enter_context(nc.semaphore(name))

        ring = sb("ring", RING * SLOT)
        xres_t = sb("xres", KT * S)
        xn_t = sb("xn", KT * S)
        mix_t = sb("mix", KT * S)
        region = sb("region", 22784)
        ident = sb("ident", P)
        ones = sb("ones", S)
        gains = sb("gains", NG)
        rinv = sb("rinv", 4 * S)
        st = sb("st", 40)
        ps = ctx.enter_context(nc.psum_tensor("ps", [P, 8, 512], f32))
        t5_dram = nc.dram_tensor("t5_table", (2 * HEADS, P, 2 * S), f32, kind="Internal")

        def tiles(t, a, n, w=S):
            return t[:, a:a + n * w].rearrange("p (t s) -> p t s", s=w)

        xres, xn, mix = tiles(xres_t, 0, KT), tiles(xn_t, 0, KT), tiles(mix_t, 0, KT)

        def R(a, n, w=S):
            return tiles(region, a, n, w)

        def gain(name, i=0):
            c = GCOL[name] + i
            return gains[:, c:c + 1]

        q1, k1, v1 = R(0, 8), R(2048, 8), R(4096, 2, 1024)
        qm, km, vm, ut = R(6144, 4), R(7168, 4), R(8192, 2, 512), R(9216, 4)
        iota = region[:, 10240:10496]
        cosb = [R(10496, 4), R(11520, 4)]
        sinb = [R(12544, 4), R(13568, 4)]
        gre, gim, t2b, tmpb = R(14592, 4), R(15616, 4), R(16640, 4), R(17664, 4)
        bbarT = R(18688, 16, P)
        cd = R(20736, 64, 32)
        bd = R(16640, 64, 32)
        decay, t1b, turns = mix[:, 0:4], mix[:, 4:8], mix[:, 12:16]
        decay_f = mix_t[:, 0:1024]
        na_bias = R(10496, 8, 512)
        na_mask = region[:, 14592:15104]
        prob1, probT1 = R(15104, 3, 512), R(16640, 2, 512)
        ga, gb, gc = R(18688, 4), R(19712, 4), R(20736, 4)
        ssm = [rinv[:, S + 32 * i:S + 32 * i + 32] for i in range(24)]
        xo, hid = R(0, KT), R(4096, FT)
        t5 = R(0, 16, 512)
        prob2, probT2 = R(8192, 3, 512), R(9728, 2, 512)
        hot, t5mask, t5tab = (region[:, 8192 + 512 * i:8704 + 512 * i] for i in range(3))
        sq_, sk_ = R(10752, 4), region[:, 11776:12032]
        small0, kpe = region[:, 12032:12288], region[:, 12288:12544]
        nq, nk, nv = R(12544, 4), R(13568, 4), R(14592, 2, 384)
        fq, fk, fv, mv = R(15360, 4), R(16384, 4), R(17408, 2, 512), R(18432, 2, 512)
        causal = region[:, 19456:19968]
        valid = region[:, 19968:19968 + TT * NCMP].rearrange("p (t c) -> p t c", c=NCMP)
        rcos, rsin = region[:, 20000:20256], region[:, 20256:20512]
        rturn = region[:, 20512:20608]
        kcp = [region[:, 20608 + 480 * i:21088 + 480 * i].rearrange("p (l c) -> p l c", c=NCMP) for i in range(2)]
        kcmp = region[:, 21568:21568 + NCMP]
        vcmp = region[0:NCMP, 21584:21712]
        ch = region[:, 21712:21776].rearrange("p (a c) -> p a c", c=16)[:, :, 0:NCMP]
        w2bd = region[:, 21776:22032].rearrange("p (a c) -> p a c", c=P)
        fc8, fneg = region[:, 22032:22288], region[:, 22288:22544]
        gates = region[:, 22544:22608].rearrange("p (t c) -> p t c", c=32)
        cpos = region[:, 22608:22672].rearrange("p (a l) -> p a l", l=CMP_LEN)
        q96, k96 = tiles(xn_t, 0, 8), tiles(xn_t, 2048, 8)

        nmax = st[:, 0:8].rearrange("p (r t) -> p r t", t=2)
        psumr = st[:, 8:16].rearrange("p (r t) -> p r t", t=2)
        pinv = st[:, 16:24].rearrange("p (r t) -> p r t", t=2)
        esink = st[:, 24:32].rearrange("p (r t) -> p r t", t=2)
        halfpi = st[:, 32:33]
        onec = st[:, 33:34]

        pe_done, act_done, dve_done, pool_done = sem("pe_done"), sem("act_done"), sem("dve_done"), sem("pool_done")
        slot_loaded = [sem(f"slot{i}_loaded") for i in range(RING)]
        acc_freed = sem("acc_freed")
        hidden_ready = sem("hidden_ready")
        small_loaded = sem("small_loaded")
        mem_loaded, x_loaded = sem("mem_loaded"), sem("x_loaded")
        ssm_loaded, na_loaded = sem("ssm_loaded"), sem("na_loaded")
        blk2_loaded, t5_in, t5_out, t5_loaded = sem("blk2_loaded"), sem("t5_in"), sem("t5_out"), sem("t5_loaded")
        out_written = sem("out_written")
        block = ctx.enter_context(nc.Block())

        def at(*name):
            return seen[name] if seen is not None else 1

        def accs(name, k=0):
            a = 2 * ((ACC0[name] + k) % 2)
            return ps[:, a:a + 2, :]

        def acc4(name, k=0):
            return accs(name, k).rearrange("p b (h s) -> p (b h) s", s=S)

        def unit(qs, ks, bias, scale, v, mix_tile, base, hd, probs, probTs, nkeys=S, sink=None, gate=None,
                 extra=None, first=True, last=True, need=()):
            return dict(qs=qs, ks=ks, bias=bias, scale=scale, v=v, mix_tile=mix_tile, base=base, hd=hd, probs=probs,
                        probTs=probTs, n=nkeys, sink=sink, gate=gate, extra=extra, first=first, last=last, need=need)

        units = []
        for h in range(MEM_HEADS):
            units.append(unit(qm[:, h], km[:, h], None, MEM_D ** -0.5, lambda kt, h=h: vm[:, kt, P * h:P * h + P],
                              12 + h, 0, P, prob1, probT1))
        for h in range(NA_HEADS):
            units.append(unit(q1[:, h], k1[:, h], na_bias[:, h], NA_D ** -0.5, lambda kt, h=h: v1[:, kt, P * h:P * h + P],
                              h, 0, P, prob1, probT1))
        U1 = len(units)
        half = lambda h: slice(64 * (h % 2), 64 * (h % 2) + 64)
        grp = lambda h: slice(64 * (h // 4), 64 * (h // 4) + 64)
        for h in range(HEADS):
            units.append(unit(sq_[grp(h), h % 4], sk_[grp(h), :], t5[:, HEADS + h], HD ** -0.5,
                              lambda kt, h=h: nv[:, kt, 256 + 64 * (h // 4):320 + 64 * (h // 4)],
                              12 + h // 2, 64 * (h % 2), HD, prob2, probT2, sink=h))
        for h in range(HEADS):
            for b in range(3):
                if b == 0:
                    cb = t5[:, h].rearrange("p (t k) -> p t k", k=S)[:, :, CMP_LEN - 1::CMP_STRIDE]
                    units.append(unit(nq[grp(h), h % 4], kcmp[grp(h), :], cb, HD ** -0.5,
                                      lambda kt, h=h: vcmp[:, 64 * (h // 4):64 * (h // 4) + 64],
                                      8 + h // 2, 64 * (h % 2), HD, prob2, probT2, nkeys=NCMP, gate=3 * h,
                                      first=True, last=False))
                else:
                    units.append(unit(nq[grp(h), h % 4], nk[grp(h), 1 + b], t5[:, h], HD ** -0.5,
                                      lambda kt, h=h, b=b: nv[:, kt, 128 * (b - 1) + 64 * (h // 4):128 * (b - 1) + 64 * (h // 4) + 64],
                                      8 + h // 2, 64 * (h % 2), HD, prob2, probT2, gate=3 * h + b,
                                      first=False, last=b == 2))
        for h in range(HEADS):
            units.append(unit(fq[half(h), h // 2], fk[half(h), h // 2], causal, HD ** -0.5,
                              lambda kt, h=h: fv[:, kt, 64 * h:64 * h + 64],
                              4 + h // 2, 64 * (h % 2), HD, prob2, probT2, extra=h))
        for h in range(HEADS):
            units.append(unit(q96[0:96, h], k96[0:96, h], causal, (NOPE + ROPE) ** -0.5,
                              lambda kt, h=h: mv[:, kt, 64 * h:64 * h + 64],
                              h // 2, 64 * (h % 2), HD, prob2, probT2))
        o_of, n_o = [], 0
        for x in units:
            o_of.append(n_o)
            n_o += x["last"]
        RANGE = {"1": (0, U1), "2": (U1, len(units))}

        def scores_ps(i, n):
            return ps[:, 4 + i % 2, 0:TT * n]

        def out_ps(i):
            x = units[i]
            o = o_of[i] % 2
            return ps[x["base"]:x["base"] + x["hd"], (7, 3)[o], 0:S]

        LOOPS = {"wout1": (16, 2, 2), "ff1_1": (16, 8, 2), "ff2_1": (64, 4, 1),
                 "wout2": (16, 2, 2), "ff1_2": (16, 8, 2), "ff2_2": (64, 4, 1)}

        @block.sync
        def _(sp):
            state = {"n": 0}

            def load(src, cols=SLOT, rows=P):
                n = state["n"]
                if n >= RING:
                    sp.wait_ge(pe_done, at("slot", n - RING))
                s = n % RING
                dst = ring[0:rows, s * SLOT:s * SLOT + cols]
                if len(src.shape) == 3:
                    dst = dst.rearrange("p (k c) -> p k c", k=src.shape[1])
                sp.dma_start(dst, src).then_inc(slot_loaded[s], 16)
                state["n"] += 1

            def rows(w, c0, width, kt0, n=SK):
                return w[kt0 * P:(kt0 + n) * P, c0:c0 + width].rearrange("(k p) c -> p k c", p=P)

            def group(w, c0, width=512):
                for j in range(KT // SK):
                    load(rows(w, c0, width, SK * j), SK * width)

            def loop(name, w):
                kts, iters, per = LOOPS[name]
                sg = kts // SK
                body = sg * per
                for j in range(body):
                    load(rows(w, 512 * (j // sg), 512, SK * (j % sg)))
                n0 = state["n"] - body
                with sp.Fori(1, iters) as i:
                    for j in range(body):
                        s = (n0 + j) % RING
                        sp.wait_ge(pe_done, at("loop", name) + body * i + (j - RING + 1))
                        kt0 = SK * (j % sg)
                        src = w[kt0 * P:(kt0 + SK) * P, bass.ds(i * (512 * per) + 512 * (j // sg), 512)]
                        sp.dma_start(ring[:, s * SLOT:(s + 1) * SLOT].rearrange("p (k c) -> p k c", k=SK),
                                     src.rearrange("(k p) c -> p k c", p=P)).then_inc(slot_loaded[s], 16)
                state["n"] = n0 + body * iters

            group(A["w_mem_kv"], 0)
            group(A["w_mem_kv"], 512)
            w = A["w_in"]
            for c0 in (3072, 0, 512, 1024, 1536, 2048, 2560, 3584):
                group(w, c0)
            load(rows(A["w_glu"], 0, 512, 0))
            loop("wout1", A["w_out"])
            loop("ff1_1", A["w_ff1"])
            loop("ff2_1", A["w_ff2"])
            w = A["w_in_2"]
            for g in range(6):
                group(w, 512 * g)
            group(w, 3072, 384)
            group(w, 3456, 512)
            for j in range(2):
                load(rows(w, 3968, 192, 8 * j, 8), 8 * 192)
            for j in range(2):
                load(A["cmp_w1"][j])
            for j in range(2):
                load(rows(A["w_uq"], 384 * j, 384, 0, 3), 3 * 384)
            load(A["w_ukv"], 1024)
            loop("wout2", A["w_out_2"])
            loop("ff1_2", A["w_up_2"])
            loop("ff2_2", A["w_down_2"])
            sp.wait_ge(dve_done, at("final", "out"))
            sp.dma_start(out, xn).then_inc(out_written, 16)
            sp.wait_ge(out_written, 16)

        @block.tensor
        def _(pe):
            m = Marks(pe, pe_done, book)
            state = {"n": 0}

            def take():
                n = state["n"]
                state["n"] += 1
                s = n % RING
                pe.wait_ge(slot_loaded[s], 16 * (n // RING + 1))
                return n, ring[:, s * SLOT:(s + 1) * SLOT]

            def acc_free(name, k=0):
                n = ACC0[name] + k
                if n >= 2:
                    pe.wait_ge(acc_freed, n - 1)

            def wide(acc, w, x, kts, kt, cols=4):
                for c in range(cols):
                    last = nc.tensor.matmul(acc[:, c], w[:, P * c:P * c + P], x, start=(kt == 0 and c % 2 == 0),
                                            stop=(kt == kts - 1), skip_group_check=True)
                return last

            def tall(acc, w, x, kts, kt, n=512):
                for t in range(TT):
                    last = nc.tensor.matmul(acc[:, t, 0:n], x[:, P * t:P * t + P], w, start=(kt == 0), stop=(kt == kts - 1))
                return last

            def group(name, x, form="wide", width=512, between=()):
                acc_free(name)
                for j in range(KT // SK):
                    n, w = take()
                    w = w[:, 0:SK * width].rearrange("p (k c) -> p k c", k=SK)
                    for k in range(SK):
                        kt = SK * j + k
                        last = (wide(acc4(name), w[:, k], x[:, kt], KT, kt) if form == "wide"
                                else tall(accs(name), w[:, k], x[:, kt], KT, kt, width))
                    m.did(last, "slot", n)
                    if j == KT // SK - 1:
                        book["acc", name] = m.n
                    for f in between:
                        f(n)

            def loop(name, x, hidden=None):
                kts, iters, per = LOOPS[name]
                sg = kts // SK
                body = sg * per
                n0, a0 = SLOT0[name], ACC0[name]
                assert n0 == state["n"]
                book["loop", name] = m.n
                with pe.Fori(0, iters) as i:
                    for j in range(body):
                        s = (n0 + j) % RING
                        g = j // sg
                        if j % sg == 0:
                            pe.wait_ge(acc_freed, i * per + (a0 + g - 1 if per == 2 else a0))
                        if hidden is not None:
                            pe.wait_ge(hidden_ready, hidden + j + 1)
                        pe.wait_ge(slot_loaded[s], i * (16 * body // RING) + 16 * ((n0 + j) // RING + 1))
                        w = ring[:, s * SLOT:(s + 1) * SLOT].rearrange("p (k c) -> p k c", k=SK)
                        for k in range(SK):
                            kt = SK * (j % sg) + k
                            last = wide(acc4(name, g), w[:, k], x[:, kt], kts, kt)
                        last.then_inc(pe_done, 1)
                for n in range(body * iters):
                    book["slot", n0 + n] = m.n + n + 1
                m.n += body * iters
                book["loop_end", name] = m.n
                state["n"] += body * iters

            def norm(name, sq, groups):
                pe.wait_ge(act_done, at(name, "sq"))
                for g, (a, n) in enumerate(groups):
                    for t in range(n):
                        last = nc.tensor.matmul(ps[:, 4 + g // 2, S * (g % 2):S * (g % 2) + S], ones[:, 0:P], sq[:, a + t],
                                                start=(t == 0), stop=(t == n - 1))
                m.did(last, name, "sum")

            def bu(i):
                if i:
                    pe.wait_ge(dve_done, at("yev", i - 1))
                d, jt = i // 4, i % 4
                x = ut[:, jt] if d == 0 else ut[:, jt, ::-1]
                for odd in range(2):
                    for j in (odd, odd + 2):
                        for part in range(2):
                            r = slice(32 * j, 32 * j + 32)
                            last = nc.tensor.matmul(ps[:, 4 + 2 * part + j // 2, S * odd:S * odd + S],
                                                    bbarT[r, 8 * part + i, :], x[r], start=True, stop=True, tile_position=(32 * j, 0))
                    m.did(last, "bu", i)
                    m.own()

            def ssm_y(i):
                pe.wait_ge(dve_done, at("h", i))
                for j in range(4):
                    o = ps[32 * j:32 * j + 32, 4, 0:S]
                    nc.tensor.matmul(o, cd[:, 4 * i + j], t1b[:, j], start=True, stop=False)
                    last = nc.tensor.matmul(o, cd[:, 32 + 4 * i + j], gim[:, j], start=False, stop=True)
                m.did(last, "y", i)

            def attention(which):
                lo, hi = RANGE[which]

                def score(i):
                    x = units[i]
                    n = x["n"]
                    if i - 2 >= lo:
                        pe.wait_ge(dve_done, at("scaled", i - 2))
                    o = scores_ps(i, n)
                    for t in range(TT):
                        ot = o[:, n * t:n * t + n]
                        ex = x["extra"]
                        last = nc.tensor.matmul(ot, x["qs"][:, P * t:P * t + P], x["ks"], start=True, stop=ex is None)
                        if ex is not None:
                            b = 64 * (ex % 2)
                            col = ident[b:b + 8, b + ex:b + ex + 1]
                            nc.tensor.matmul(ot, fc8[b:b + 8, P * t:P * t + P], col.to_broadcast([8, S]), start=False, stop=False)
                            last = nc.tensor.matmul(ot, col.to_broadcast([8, P]), fneg[b:b + 8, :], start=False, stop=True)
                    m.did(last, "scores", i)

                def turn(i):
                    x = units[i]
                    n = x["n"]
                    pe.wait_ge(dve_done, at("probs", i))
                    if i - 2 >= lo:
                        pe.wait_ge(act_done, at("probT", i - 2))
                    p = x["probs"][:, i % 3]
                    for kt in range(max(1, n // P)):
                        for t in range(TT):
                            w = min(P, n)
                            last = nc.tensor.transpose(ps[0:w, (6, 2)[i % 2], S * kt + P * t:S * kt + P * t + P],
                                                       p[:, n * t + P * kt:n * t + P * kt + w], ident[:, :])
                    m.did(last, "turned", i)

                def value(i):
                    x = units[i]
                    pe.wait_ge(act_done, at("probT", i))
                    if x["first"] and o_of[i] - 2 >= o_of[lo]:
                        pe.wait_ge(act_done, at("out", o_of[i] - 2))
                    nkt = max(1, x["n"] // P)
                    for kt in range(nkt):
                        last = nc.tensor.matmul(out_ps(i), x["v"](kt), x["probTs"][0:min(P, x["n"]), i % 2, S * kt:S * kt + S],
                                                start=(kt == 0 and x["first"]), stop=(kt == nkt - 1 and x["last"]))
                    m.did(last, "value", i)

                for i in range(lo, hi + 3):
                    if i < hi:
                        score(i)
                    if lo <= i - 2 < hi:
                        turn(i - 2)
                    if lo <= i - 3:
                        value(i - 3)

            pe.wait_ge(small_loaded, 32)
            pe.wait_ge(dve_done, at("ones"))
            norm("mem", xn, [(0, KT)])
            pe.wait_ge(dve_done, at("mem", "sumread"))
            norm("x", R(0, KT), [(0, KT)])
            pe.wait_ge(dve_done, at("mem", "out"))
            group("memk", mix)
            group("memv", mix, "tall")
            pe.wait_ge(dve_done, at("x", "out"))
            group("u", xn)
            pe.wait_ge(dve_done, at("bbar"))
            pe.wait_ge(dve_done, at("x", "sumread"))
            for part, src in enumerate((gre, gim)):
                src = src.rearrange("p t s -> p (t s)")
                for k in range(8):
                    o = 8 * part + k
                    last = nc.tensor.transpose(ps[:, 4 + o // 4, P * (o % 4):P * (o % 4) + P], src[:, P * k:P * k + P], ident[:, :])
            m.did(last, "bbar_turned")
            first = state["n"]
            due = {first + (7 * i) // 2: i for i in range(CHUNKS)}

            def ssm_steps(n):
                if n + 1 in due and due[n + 1]:
                    ssm_y(due[n + 1] - 1)
                if n in due:
                    if due[n] == 0:
                        pe.wait_ge(act_done, at("bbarT"))
                        pe.wait_ge(act_done, at("evac", "u"))
                    bu(due[n])

            for g in ("q0", "q1", "k0", "k1"):
                group(g, xn, between=[ssm_steps])
            for g in ("v0", "v1"):
                group(g, xn, "tall", between=[ssm_steps])
            group("qm", xn, between=[ssm_steps])
            ssm_y(CHUNKS - 1)
            pe.wait_ge(dve_done, at("gelu"))
            acc_free("glu")
            n, w = take()
            w = w.rearrange("p (k c) -> p k c", k=SK)
            for k in range(SK):
                last = wide(acc4("glu"), w[:, k], ga[:, k], SK, k)
            m.did(last, "slot", n)
            book["acc", "glu"] = m.n
            pe.wait_ge(act_done, at("evac", "qm"))
            pe.wait_ge(dve_done, at("yev", CHUNKS - 1))
            attention("1")
            norm("outn", xn, [(0, 8), (8, 4), (12, 4)])
            pe.wait_ge(dve_done, at("outn", "out"))
            loop("wout1", mix)
            norm("post", xn, [(0, KT)])
            norm("mlp", mix, [(0, KT)])
            pe.wait_ge(dve_done, at("mlp", "out"))
            loop("ff1_1", xn)
            loop("ff2_1", hid, hidden=0)
            norm("mpost", xn, [(0, KT)])
            norm("attn2", mix, [(0, KT)])

            pe.wait_ge(dve_done, at("attn2", "out"))
            for g in W2_GROUPS[:-1]:
                group(g, xn, "tall" if g in ("fv", "nv") else "wide", 384 if g == "nv" else 512)
                if g == "mla_c":
                    pe.wait_ge(t5_in, 32)
                    m.did(nc.tensor.matmul(ps[0:2 * HEADS, 6, :], rinv[0:BUCKETS, S:S + 2 * HEADS], hot[0:BUCKETS, :],
                                           start=True, stop=True), "t5_table")
            acc_free("small")
            a = acc4("small")
            for j in range(2):
                n, w = take()
                w = w[:, 0:8 * 192].rearrange("p (k c) -> p k c", k=8)
                for k in range(8):
                    kt = 8 * j + k
                    nc.tensor.matmul(a[:, 0], w[:, k, 0:P], xn[:, kt], start=(kt == 0), stop=(kt == KT - 1), skip_group_check=True)
                    nc.tensor.matmul(a[0:64, 1], w[:, k, P:P + 64], xn[:, kt], start=False, stop=(kt == KT - 1), skip_group_check=True)
                    nc.tensor.matmul(a[64:128, 1], w[:, k, P:P + 64], xn[:, kt], start=False, stop=(kt == KT - 1), skip_group_check=True)
                    last = nc.tensor.matmul(a[64:96, 2], w[:, k, P + 32:P + 64], xn[:, kt], start=(kt == 0), stop=(kt == KT - 1), skip_group_check=True)
                m.did(last, "slot", n)
            book["acc", "small"] = m.n
            for b, name in enumerate(("cmpk", "cmpv")):
                pe.wait_ge(dve_done, at("kcp", b))
                acc_free(name)
                n, w = take()
                w = w.rearrange("p (l c) -> p l c", l=CMP_LEN)
                for g in range(2):
                    r = slice(64 * g, 64 * g + 64)
                    for l in range(CMP_LEN):
                        last = nc.tensor.matmul(accs(name)[r, g, 0:NCMP], w[r, l], kcp[b][r, l], start=(l == 0), stop=(l == CMP_LEN - 1))
                m.did(last, "slot", n)
                book["acc", name] = m.n
                pe.wait_ge(dve_done, at("cmp_gelu", b))
                pe.wait_ge(blk2_loaded, 48)
                acc_free(name + "2")
                if b == 0:
                    m.did(nc.tensor.matmul(accs(name + "2")[:, 0, 0:NCMP], w2bd[:, b], ch[:, 3], start=True, stop=True), "acc", name + "2")
                else:
                    m.did(nc.tensor.matmul(accs(name + "2")[0:NCMP, 0, 0:P], ch[:, 3], w2bd[:, b], start=True, stop=True), "acc", name + "2")
            norm("mlan", mix[:, 4:8], [(0, 3), (3, 1)])
            pe.wait_ge(dve_done, at("mlan", "out"))
            for b, name in enumerate(("uqa", "uqb")):
                acc_free(name)
                n, w = take()
                w = w[:, 0:3 * 384].rearrange("p (k c) -> p k c", k=3)
                for h in range(4):
                    for k in range(3):
                        last = nc.tensor.matmul(acc4(name)[0:96, h], w[:, k, 96 * h:96 * h + 96], mix[:, k], start=(k == 0), stop=(k == 2))
                m.did(last, "slot", n)
                book["acc", name] = m.n
                pe.wait_ge(act_done, at("evac", name))
                acc_free(name + "r")
                for c in range(2):
                    last = nc.tensor.matmul(accs(name + "r")[0:96, c], rturn[0:96, :], q96[0:96, 4 * b + 2 * c:4 * b + 2 * c + 2],
                                            start=True, stop=True)
                m.did(last, "acc", name + "r")
            acc_free("kper")
            pe.wait_ge(act_done, at("evac", "small"))
            m.did(nc.tensor.matmul(accs("kper")[0:96, 0, 0:S], rturn[64:96, :], kpe[64:96, :], start=True, stop=True), "acc", "kper")
            n, w = take()
            for b, name in enumerate(("kna", "knb")):
                acc_free(name)
                for h in range(4):
                    last = nc.tensor.matmul(acc4(name)[0:64, h], w[:, 64 * (4 * b + h):64 * (4 * b + h) + 64], mix[:, 3], start=True, stop=True)
                m.did(last, "acc", name)
            acc_free("mv")
            last = tall(accs("mv"), w[:, 512:1024], mix[:, 3], 1, 0)
            m.did(last, "slot", n)
            book["acc", "mv"] = m.n
            pe.wait_ge(dve_done, at("mlan", "sumread"))
            for t in range(TT):
                last = nc.tensor.transpose(ps[:, 6, 32 * t:32 * t + 32], small0[0:32, P * t:P * t + P], ident[0:32, 0:32])
            m.did(last, "gates_turned")
            pe.wait_ge(act_done, at("gates"))
            pe.wait_ge(dve_done, at("ready2"))
            pe.wait_ge(act_done, at("evac", "mv"))
            attention("2")
            norm("group", xn, [(0, 4), (4, 4), (8, 4), (12, 4)])
            pe.wait_ge(dve_done, at("group", "out"))
            loop("wout2", mix)
            norm("mlp2", mix, [(0, KT)])
            pe.wait_ge(dve_done, at("mlp2", "out"))
            loop("ff1_2", xn)
            loop("ff2_2", hid, hidden=16)
            norm("final", mix, [(0, KT)])

        @block.scalar
        def _(act):
            m = Marks(act, act_done, book)

            def square(name, src, dst):
                m.did(nc.scalar.activation(dst, src, ACT.Square), name, "sq")

            def root(name, groups):
                act.wait_ge(dve_done, at(name, "rec"))
                r = rinv[:, 0:groups * S]
                m.did(nc.scalar.activation(r, r, ACT.Sqrt), name, "rinv")

            def evac(name, dst, src=None, bias=None):
                act.wait_ge(pe_done, at("acc", name))
                src = acc4(name) if src is None else src
                nc.scalar.activation(dst, src, ACT.Copy).then_inc(acc_freed, 1)
                act.wait_ge(acc_freed, ACC0[name] + 1)
                m.own()
                m.did(nc.scalar.activation(st[:, 36:37], onec, ACT.Copy), "evac", name)

            def evac_loop(name, relu=None):
                kts, iters, per = LOOPS[name]
                sg = kts // SK
                body = sg * per
                with act.Fori(0, iters) as i:
                    for g in range(per):
                        act.wait_ge(pe_done, i * body + (at("loop", name) + sg * (g + 1)))
                        act.wait_ge(small_loaded, 32)
                        dst = (xo_flat if relu is None else hid_flat)[:, bass.ds(i * (per * 1024) + 1024 * g, 1024)]
                        src = accs(name, g).rearrange("p b c -> p (b c)")
                        nc.scalar.activation(dst, src, ACT.Copy if relu is None else ACT.Relu).then_inc(acc_freed, 1)

            xo_flat = region[:, 0:4096]
            hid_flat = region[:, 4096:4096 + FT * S]

            def attention(which):
                lo, hi = RANGE[which]

                def exps(i):
                    x = units[i]
                    n = x["n"]
                    act.wait_ge(dve_done, at("max", i))
                    m.own()
                    r = i % 4
                    if x["sink"] is not None:
                        m.did(nc.scalar.activation(esink[:, r], nmax[:, r], ACT.Exp, bias=gain("sinks", x["sink"])))
                    for t in range(TT):
                        s = x["probs"][:, i % 3, n * t:n * t + n]
                        last = nc.scalar.activation(s, s, ACT.Exp, bias=nmax[:, r, t:t + 1], accum_out=psumr[:, r, t:t + 1])
                        m.did(last, "exp", i)

                def turned(i):
                    x = units[i]
                    act.wait_ge(pe_done, at("turned", i))
                    if i - 2 >= lo:
                        act.wait_ge(pe_done, at("value", i - 2))
                    w, c = (P, 512) if x["n"] == S else (x["n"], S)
                    m.did(nc.scalar.activation(x["probTs"][0:w, i % 2, 0:c], ps[0:w, (6, 2)[i % 2], 0:c], ACT.Copy), "probT", i)

                def outs(i):
                    x = units[i]
                    if not x["last"]:
                        return
                    act.wait_ge(pe_done, at("value", i))
                    m.did(nc.scalar.activation(mix[x["base"]:x["base"] + x["hd"], x["mix_tile"]], out_ps(i), ACT.Copy), "out", o_of[i])

                for i in range(lo, hi + 4):
                    if i < hi:
                        exps(i)
                    if lo <= i - 2 < hi:
                        turned(i - 2)
                    if lo <= i - 4:
                        outs(i - 4)

            act.dma_start(ident[:, :], A["ident"]).then_inc(small_loaded, 16)
            act.dma_start(gains[:, :], A["gains"]).then_inc(small_loaded, 16)
            act.dma_start(mix[:, :, :], A["memT"]).then_inc(mem_loaded, 16)
            act.dma_start(xres[:, :, :], A["xT"]).then_inc(x_loaded, 16)
            act.dma_start(rinv[:, S:S + 96], A["ssm_p"]).then_inc(ssm_loaded, 16)
            act.dma_start(bd, A["ssm_b"]).then_inc(ssm_loaded, 16)
            act.dma_start(cd, A["ssm_c"]).then_inc(ssm_loaded, 16)
            act.dma_start(iota, A["iota"]).then_inc(ssm_loaded, 16)
            act.wait_ge(mem_loaded, 16)
            square("mem", mix[:, :, :], xn[:, :, :])
            act.wait_ge(x_loaded, 16)
            square("x", xres[:, :, :], R(0, KT))
            root("mem", 1)
            root("x", 1)
            act.wait_ge(ssm_loaded, 64)
            dt, mag, s1, c1 = ssm[3], ssm[4], ssm[5], ssm[6]
            m.did(nc.scalar.activation(dt, ssm[2], ACT.Exp), "dt")
            act.wait_ge(dve_done, at("lrdt"))
            m.did(nc.scalar.activation(mag, ssm[7], ACT.Exp), "mag")
            act.wait_ge(dve_done, at("frac"))
            m.did(nc.scalar.activation(s1, ssm[8], ACT.Sin, scale=6.283185))
            m.did(nc.scalar.activation(c1, ssm[9], ACT.Sin, scale=-6.283185, bias=halfpi), "sc1")
            evac("memk", km)
            evac("memv", vm, accs("memv"))
            evac("u", ut)
            act.wait_ge(pe_done, at("bbar_turned"))
            m.did(nc.scalar.activation(bbarT.rearrange("p a s -> p (a s)"), ps[:, 4:8, :].rearrange("p b c -> p (b c)"), ACT.Copy), "bbarT")

            def tables(i):
                act.wait_ge(pool_done, at("turns", i))
                if i >= 2:
                    act.wait_ge(dve_done, at("h", i - 2))
                else:
                    act.wait_ge(dve_done, at("bbar"))
                m.did(nc.scalar.activation(sinb[i % 2], turns, ACT.Sin, scale=6.283185))
                m.own()
                m.did(nc.scalar.activation(turns, turns, ACT.Abs))
                m.own()
                m.did(nc.scalar.activation(cosb[i % 2], turns, ACT.Sin, scale=-6.283185, bias=halfpi), "tables", i)

            tables(0)
            tables(1)
            for c, (name, dst, src) in enumerate([("q0", q1[:, 0:4], None), ("q1", q1[:, 4:8], None), ("k0", k1[:, 0:4], None), ("k1", k1[:, 4:8], None),
                                    ("v0", v1[:, :, 0:512], accs("v0")), ("v1", v1[:, :, 512:1024], accs("v1")),
                                    ("qm", qm, None)]):
                if c + 2 < CHUNKS:
                    tables(c + 2)
                evac(name, dst, src)
            act.wait_ge(dve_done, at("gelu_in"))
            m.did(nc.scalar.activation(gb, gb, ACT.Tanh, scale=0.7978845608028654), "gelu_tanh")
            act.wait_ge(pe_done, at("acc", "glu"))
            act.wait_ge(dve_done, at("half_b"))
            for c in range(4):
                last = nc.scalar.activation(gb[:, c], acc4("glu")[:, c], ACT.Tanh, scale=0.5, bias=gc[:, c, 0:1])
                if c < 3:
                    m.did(last)
                else:
                    last.then_inc(acc_freed, 1)
            act.wait_ge(acc_freed, ACC0["glu"] + 1)
            m.own()
            m.did(nc.scalar.activation(st[:, 36:37], onec, ACT.Copy), "glu_gate")
            act.wait_ge(dve_done, at("h", CHUNKS - 1))
            act.wait_ge(pe_done, at("y", CHUNKS - 1))
            act.dma_start(na_mask, A["na_mask"]).then_inc(na_loaded, 16)
            rpb = A["na_rpb"]
            for r in range(S // GRID_W):
                for rk in range(S // GRID_W):
                    src = bass.AP(rpb.tensor, (rk - r + WIN_H - 1) * RPB_W + WIN_W - 1, [[NA_HEADS * RPB_H * RPB_W - 1, GRID_W], [RPB_H * RPB_W, NA_HEADS], [1, GRID_W]])
                    c0 = S * (r // 2) + GRID_W * rk
                    act.dma_start(na_bias[64 * (r % 2):64 * (r % 2) + 64, :, c0:c0 + GRID_W], src).then_inc(na_loaded, 16)
            attention("1")
            m.own()
            act.wait_ge(dve_done, at("ssm_out"))
            square("outn", mix[:, :, :], xn[:, :, :])
            root("outn", 3)
            evac_loop("wout1")
            act.wait_ge(acc_freed, ACC0["wout1"] + 4)
            square("post", R(0, KT), xn[:, :, :])
            root("post", 1)
            act.wait_ge(dve_done, at("post", "added"))
            square("mlp", xres[:, :, :], mix[:, :, :])
            root("mlp", 1)
            evac_loop("ff1_1", relu=True)
            evac_loop("ff2_1")
            act.wait_ge(acc_freed, ACC0["ff2_1"] + 4)
            square("mpost", R(0, KT), xn[:, :, :])
            root("mpost", 1)
            act.wait_ge(dve_done, at("mpost", "added"))
            square("attn2", xres[:, :, :], mix[:, :, :])
            root("attn2", 1)

            act.wait_ge(dve_done, at("attn2", "out"))
            act.dma_start(hot, A["t5"][:, 0:512]).then_inc(t5_in, 16)
            act.dma_start(rinv[0:BUCKETS, S:S + 2 * HEADS], A["rel"]).then_inc(t5_in, 16)
            act.dma_start(t5mask, A["t5"][:, 512:1024]).then_inc(blk2_loaded, 16)
            act.dma_start(region[:, 19456:20608], A["block2"]).then_inc(blk2_loaded, 16)
            act.dma_start(region[:, 21776:22032], A["cmp_w2"]).then_inc(blk2_loaded, 16)
            act.dma_start(region[:, 22608:22672], A["cmp_pos"]).then_inc(blk2_loaded, 16)
            evac("mla_c", mix[:, 0:4])
            act.wait_ge(dve_done, at("t5_masked"))
            act.dma_start(t5_dram.ap(), t5tab[0:2 * HEADS, :].unsqueeze(1).to_broadcast([2 * HEADS, P, 2 * S])).then_inc(t5_out, 16)
            act.wait_ge(t5_out, 16)
            for t in range(TT):
                src = bass.AP(t5_dram.ap().tensor, S - 1 - P * t, [[2 * S - 1, P], [2 * S * P, 2 * HEADS], [1, S]])
                act.dma_start(t5[:, :, S * t:S * t + S], src).then_inc(t5_loaded, 16)
            m.own()
            square("mlan", mix[:, 0:4], mix[:, 4:8])
            for name, dst, src in [("fq", fq, None), ("fk", fk, None), ("fv", fv, accs("fv")), ("nq", nq, None), ("nk", nk, None),
                                   ("nv", nv, accs("nv")[:, :, 0:384]), ("sq", sq_, None)]:
                evac(name, dst, src)
            act.wait_ge(pe_done, at("acc", "small"))
            m.did(nc.scalar.activation(sk_, acc4("small")[:, 0], ACT.Copy))
            m.did(nc.scalar.activation(small0, acc4("small")[:, 1], ACT.Identity, bias=gain("b_f")), "small0")
            nc.scalar.activation(kpe[64:96, :], acc4("small")[64:96, 2], ACT.Copy).then_inc(acc_freed, 1)
            act.wait_ge(acc_freed, ACC0["small"] + 1)
            m.own()
            m.did(nc.scalar.activation(st[:, 36:37], onec, ACT.Copy), "evac", "small")
            for b, name in enumerate(("cmpk", "cmpv")):
                act.wait_ge(pe_done, at("acc", name))
                if b:
                    act.wait_ge(pe_done, at("acc", "cmpk2"))
                m.did(nc.scalar.activation(ch[0:64, 0], accs(name)[0:64, 0, 0:NCMP], ACT.Copy))
                nc.scalar.activation(ch[64:128, 0], accs(name)[64:128, 1, 0:NCMP], ACT.Copy).then_inc(acc_freed, 1)
                act.wait_ge(acc_freed, ACC0[name] + 1)
                m.own()
                m.did(nc.scalar.activation(st[:, 36:37], onec, ACT.Copy), "evac", name)
                act.wait_ge(dve_done, at("cmp_in", b))
                m.did(nc.scalar.activation(ch[:, 1], ch[:, 1], ACT.Tanh, scale=0.7978845608028654), "cmp_tanh", b)
                if b == 0:
                    evac("cmpk2", kcmp, accs("cmpk2")[:, 0, 0:NCMP])
                else:
                    evac("cmpv2", vcmp, accs("cmpv2")[0:NCMP, 0, 0:P])
            root("mlan", 2)
            act.wait_ge(dve_done, at("f_abs"))
            m.did(nc.scalar.activation(fneg, fneg, ACT.Exp, scale=-1.0))
            m.own()
            m.did(nc.scalar.activation(fneg, fneg, ACT.Ln, bias=onec), "f_ln")
            for b, name in enumerate(("uqa", "uqb")):
                evac(name, q96[0:96, 4 * b:4 * b + 4], acc4(name)[0:96])
                evac(name + "r", k96[0:96, 4 * b:4 * b + 4], acc4(name + "r")[0:96])
            act.wait_ge(dve_done, at("kcp", 1))
            act.wait_ge(pe_done, at("acc", "cmpv"))
            evac("kper", region[64:96, 20608:20864], accs("kper")[64:96, 0, 0:S])
            for b, name in enumerate(("kna", "knb")):
                act.wait_ge(dve_done, at("q96", b))
                evac(name, k96[0:64, 4 * b:4 * b + 4], acc4(name)[0:64])
            evac("mv", mv, accs("mv"))
            act.wait_ge(pe_done, at("gates_turned"))
            m.did(nc.scalar.activation(gates, ps[:, 6, 0:64].rearrange("p (t c) -> p t c", c=32), ACT.Tanh, scale=0.5), "gates")
            act.wait_ge(dve_done, at("ready2"))
            attention("2")
            m.own()
            square("group", mix[:, :, :], xn[:, :, :])
            root("group", 4)
            evac_loop("wout2")
            act.wait_ge(dve_done, at("wout2", "added"))
            square("mlp2", xres[:, :, :], mix[:, :, :])
            root("mlp2", 1)
            evac_loop("ff1_2", relu=True)
            evac_loop("ff2_2")
            act.wait_ge(dve_done, at("ff2_2", "added"))
            square("final", xres[:, :, :], mix[:, :, :])
            root("final", 1)

        @block.gpsimd
        def _(pool):
            m = Marks(pool, pool_done, book)
            MAGIC = 12582912.0
            pool.wait_ge(dve_done, at("frac"))
            pool.wait_ge(ssm_loaded, 64)
            pool.wait_ge(pe_done, at("acc", "memv"))
            pool.wait_ge(dve_done, at("bbar"))
            time = iota.unsqueeze(1).to_broadcast([P, 4, S])
            for i in range(CHUNKS):
                col = lambda k: ssm[k][:, 4 * i:4 * i + 4].unsqueeze(2).to_broadcast([P, 4, S])
                if i:
                    pool.wait_ge(act_done, at("tables", i - 1))
                m.did(nc.gpsimd.tensor_tensor(tmpb, time, col(8), ALU.mult))
                m.own()
                m.did(nc.gpsimd.tensor_scalar(tmpb, tmpb, MAGIC, MAGIC, ALU.add, ALU.subtract))
                m.did(nc.gpsimd.tensor_tensor(turns, time, col(10), ALU.mult))
                m.own()
                m.did(nc.gpsimd.tensor_tensor(turns, turns, tmpb, ALU.subtract))
                m.own()
                m.did(nc.gpsimd.tensor_tensor(tmpb, time, col(11), ALU.mult))
                m.own()
                m.did(nc.gpsimd.tensor_tensor(turns, turns, tmpb, ALU.add))
                m.own()
                m.did(nc.gpsimd.tensor_scalar(turns, turns, 0.5, -0.5, ALU.min, ALU.max), "turns", i)

        @block.vector
        def _(dve):
            m = Marks(dve, dve_done, book)
            V = nc.vector

            def tt(o, a, b, op, *name):
                m.did(V.tensor_tensor(o, a, b, op), *name)

            def moments(name, dims):
                dve.wait_ge(pe_done, at(name, "sum"))
                m.own()
                for g, d in enumerate(dims):
                    last = V.tensor_scalar(rinv[:, S * g:S * g + S], ps[:, 4 + g // 2, S * (g % 2):S * (g % 2) + S],
                                           1.0 / d, EPS, ALU.mult, ALU.add)
                    m.did(last, name, "sumread")
                m.own()
                r = rinv[:, 0:len(dims) * S]
                m.did(V.reciprocal(r, r), name, "rec")

            def scaled(name, src, dst, g, n, a=0, col=None):
                dve.wait_ge(act_done, at(name, "rinv"))
                m.own()
                for t in range(n):
                    m.did(V.scalar_tensor_tensor(dst[:, a + t], src[:, a + t], gain(col or name, a + t), rinv[:, S * g:S * g + S],
                                                 ALU.mult, ALU.mult), name, "out")

            def attention(which, between=()):
                lo, hi = RANGE[which]

                def scale(i):
                    x = units[i]
                    n, r = x["n"], i % 4
                    dve.wait_ge(pe_done, at("scores", i))
                    if i - 3 >= lo:
                        dve.wait_ge(pe_done, at("turned", i - 3))
                    if i - 4 >= lo:
                        dve.wait_ge(act_done, at("exp", i - 4))
                    m.own()
                    s = x["probs"][:, i % 3, 0:TT * n]
                    if x["bias"] is None:
                        ins = V.tensor_scalar(s, scores_ps(i, n), x["scale"], None, ALU.mult)
                    elif n == S:
                        ins = V.scalar_tensor_tensor(s, scores_ps(i, n), x["scale"], x["bias"], ALU.mult, ALU.add)
                    else:
                        k3 = lambda a: a.rearrange("p (t k) -> p t k", k=n)
                        ins = V.scalar_tensor_tensor(k3(s), k3(scores_ps(i, n)), x["scale"], x["bias"], ALU.mult, ALU.add)
                    m.did(ins, "scaled", i)
                    m.own()
                    m.did(V.tensor_reduce(nmax[:, r], s.rearrange("p (t k) -> p t k", k=n), AX.X, ALU.max, negate=True), "max", i)
                    if x["sink"] is not None:
                        m.own()
                        m.did(V.tensor_scalar(nmax[:, r], nmax[:, r], negsink[:, x["sink"]:x["sink"] + 1], None, ALU.min), "max", i)

                def normal(i):
                    x = units[i]
                    n, r = x["n"], i % 4
                    dve.wait_ge(act_done, at("exp", i))
                    if x["sink"] is not None:
                        tt(psumr[:, r], psumr[:, r], esink[:, r], ALU.add)
                        m.own()
                    m.did(V.reciprocal(pinv[:, r], psumr[:, r]))
                    m.own()
                    if x["gate"] is not None:
                        tt(pinv[:, r], pinv[:, r], gates[:, :, 8 + x["gate"]], ALU.mult)
                        m.own()
                    for t in range(TT):
                        s = x["probs"][:, i % 3, n * t:n * t + n]
                        if n == S:
                            ins = V.tensor_scalar(s, s, pinv[:, r, t:t + 1], None, ALU.mult)
                        else:
                            ins = V.scalar_tensor_tensor(s, s, pinv[:, r, t:t + 1], valid[:, t], ALU.mult, ALU.mult)
                        m.did(ins, "probs", i)

                for i in range(lo, hi + 1):
                    if i < hi:
                        scale(i)
                    if lo <= i - 1:
                        normal(i - 1)
                    for f in between:
                        f(i)

            V.memset(ones[:, :], 1.0)
            V.memset(halfpi, float(np.float32(np.pi / 2)))
            m.did(V.memset(onec, 1.0), "ones")
            dve.wait_ge(small_loaded, 32)
            moments("mem", [D])
            scaled("mem", mix, mix, 0, KT)
            moments("x", [D])
            scaled("x", xres, xn, 0, KT, col="mix_pre")
            dve.wait_ge(ssm_loaded, 64)
            dve.wait_ge(act_done, at("dt"))
            lr, li, dt, mag, s1, c1 = ssm[0], ssm[1], ssm[3], ssm[4], ssm[5], ssm[6]
            lrdt, f, af, fhi, flo, th, nn, a1, a2, a3, wr, wi = ssm[7:19]
            MAGIC = 12582912.0
            ts = lambda o, a, x, y, p, q=None: m.did(V.tensor_scalar(o, a, x, y, p, q) if q is not None else V.tensor_scalar(o, a, x, None, p))
            ts(lr, lr, LAM_MAX, None, ALU.min)
            m.own()
            tt(lrdt, lr, dt, ALU.mult, "lrdt")
            tt(th, li, dt, ALU.mult)
            m.own()
            ts(nn, th, float(np.float32(1 / (2 * np.pi))), MAGIC, ALU.mult, ALU.add)
            m.own()
            ts(nn, nn, MAGIC, None, ALU.subtract)
            m.own()
            c_hi = 6.28125
            c_mid = float(np.float32(2 * np.pi - c_hi))
            c_lo = float(np.float32(2 * np.pi - c_hi - c_mid))
            for c in (c_hi, c_mid, c_lo):
                m.did(V.scalar_tensor_tensor(th, nn, -c, th, ALU.mult, ALU.add))
                m.own()
            ts(f, th, float(np.float32(1 / (2 * np.pi))), None, ALU.mult)
            m.own()
            ts(f, f, 0.5, -0.5, ALU.min, ALU.max)
            m.own()
            m.did(V.scalar_tensor_tensor(af, f, -1.0, f, ALU.mult, ALU.max))
            ts(fhi, f, 192.0, 192.0, ALU.add, ALU.subtract)
            m.own()
            tt(flo, f, fhi, ALU.subtract, "frac")
            dve.wait_ge(act_done, at("sc1"))
            tt(a1, mag, c1, ALU.mult)
            tt(a2, mag, s1, ALU.mult)
            m.own()
            ts(a1, a1, -1.0, None, ALU.add)
            tt(nn, lr, lr, ALU.mult)
            tt(th, li, li, ALU.mult)
            m.own()
            tt(nn, nn, th, ALU.add)
            m.own()
            m.did(V.reciprocal(nn, nn))
            tt(wr, a1, lr, ALU.mult)
            tt(th, a2, li, ALU.mult)
            tt(wi, a2, lr, ALU.mult)
            tt(a3, a1, li, ALU.mult)
            m.own()
            tt(wr, wr, th, ALU.add)
            tt(wi, wi, a3, ALU.subtract)
            m.own()
            tt(wr, wr, nn, ALU.mult)
            tt(wi, wi, nn, ALU.mult)
            m.own()
            wide32 = lambda a: a.unsqueeze(2).to_broadcast([P, 32, 32])
            bre, bim = bd[:, 0:32], bd[:, 32:64]
            v32 = lambda a: a.rearrange("p t s -> p (t s)").rearrange("p (a b) -> p a b", b=32)
            br, bi, x1, x2 = v32(gre), v32(gim), v32(cosb[0]), v32(cosb[1])
            tt(br, bre, wide32(wr), ALU.mult)
            tt(x1, bim, wide32(wi), ALU.mult)
            tt(bi, bim, wide32(wr), ALU.mult)
            tt(x2, bre, wide32(wi), ALU.mult)
            m.own()
            tt(br, br, x1, ALU.subtract)
            tt(bi, bi, x2, ALU.add, "bbar")
            ts(cd[:, 32:64], cd[:, 32:64], -1.0, None, ALU.mult)
            dve.wait_ge(pe_done, at("acc", "memv"))

            def decays(i):
                m.did(V.tensor_copy(decay, mag[:, 4 * i:4 * i + 4].unsqueeze(2).to_broadcast([P, 4, S])))
                m.own()
                m.did(V.memset(decay[:, :, 0:1], 0.0))

            flat = lambda a: a.rearrange("p t s -> p (t s)")
            decays(0)
            for i in range(CHUNKS):
                cs, sn = cosb[i % 2], sinb[i % 2]
                bur = ps[:, 4:6, :].rearrange("p b (h s) -> p (b h) s", s=S)
                bui = ps[:, 6:8, :].rearrange("p b (h s) -> p (b h) s", s=S)
                dve.wait_ge(pe_done, at("bu", i))
                m.own()
                dve.wait_ge(act_done, at("tables", i))
                if i == 0:
                    dve.wait_ge(act_done, at("bbarT"))
                tt(t1b, bur, cs, ALU.mult)
                tt(t2b, bui, sn, ALU.mult)
                m.own()
                tt(gre, t1b, t2b, ALU.add)
                m.own()
                tt(t1b, bui, cs, ALU.mult)
                tt(t2b, bur, sn, ALU.mult)
                m.own()
                tt(gim, t1b, t2b, ALU.subtract)
                m.own()
                for g in (gre, gim):
                    m.did(V.tensor_tensor_scan(flat(g), decay_f, flat(g), 0.0, ALU.mult, ALU.add))
                m.own()
                tt(t1b, cs, gre, ALU.mult)
                tt(t2b, sn, gim, ALU.mult)
                m.own()
                tt(t1b, t1b, t2b, ALU.subtract)
                m.own()
                tt(t2b, sn, gre, ALU.mult)
                m.own()
                tt(gim, cs, gim, ALU.mult)
                m.own()
                tt(gim, t2b, gim, ALU.add, "h", i)
                if i + 1 < CHUNKS:
                    decays(i + 1)
                d, jt = i // 4, i % 4
                dve.wait_ge(pe_done, at("y", i))
                m.own()
                yp = ps[:, 4, 0:S]
                o = mix[:, 8 + jt]
                if d == 0:
                    m.did(V.scalar_tensor_tensor(o, ut[:, jt], gain("ssm_d", jt), yp, ALU.mult, ALU.add), "yev", i)
                else:
                    tt(o, ps[:, 4, S - 1::-1][:, 0:S] if False else yp[:, ::-1], o, ALU.add, "yev", i)
            y = mix[:, 8:12]
            m.own()
            tt(ga, y, y, ALU.mult)
            m.own()
            ts(ga, ga, 0.044715, 1.0, ALU.mult, ALU.add)
            m.own()
            tt(gb, ga, y, ALU.mult, "gelu_in")
            dve.wait_ge(act_done, at("gelu_tanh"))
            m.did(V.scalar_tensor_tensor(ga, gb, 1.0, y, ALU.add, ALU.mult))
            m.own()
            ts(ga, ga, 0.5, None, ALU.mult)
            book["gelu",] = m.n
            ts(gc[:, :, 0:1], gains[:, GCOL["b_glu"]:GCOL["b_glu"] + 4].unsqueeze(2), 0.5, None, ALU.mult)
            book["half_b",] = m.n
            dve.wait_ge(act_done, at("glu_gate"))
            m.did(V.scalar_tensor_tensor(gb, gb, 1.0, ga, ALU.add, ALU.mult))
            m.own()
            ts(y, gb, 0.5, None, ALU.mult)
            book["ssm_out",] = m.n
            negsink = gains[:, GCOL["sinks"]:GCOL["sinks"] + 8]

            def add_mask(i):
                if i == MEM_HEADS - 1:
                    dve.wait_ge(na_loaded, 16 * 17)
                    m.did(V.tensor_tensor(na_bias, na_bias, na_mask.unsqueeze(1).to_broadcast([P, 8, 512]), ALU.add))
                    m.own()

            attention("1", [add_mask])
            moments("outn", [1024, 512, 512])
            scaled("outn", mix, mix, 0, 8, 0, "out")
            scaled("outn", mix, mix, 1, 4, 8, "out")
            scaled("outn", mix, mix, 2, 4, 12, "out")

            def post(name, col):
                moments(name, [D])
                scaled(name, xo, xo, 0, KT, col=col)
                m.own()
                tt(xres, xres, xo, ALU.add, name, "added")

            def squares(name):
                kts, iters, per = LOOPS[name]
                with dve.Fori(0, iters) as i:
                    for g in range(per):
                        h = region[:, 4096:4096 + FT * S][:, bass.ds(i * (per * 1024) + 1024 * g, 1024)]
                        dve.wait_ge(acc_freed, i * per + (ACC0[name] + g + 1))
                        V.tensor_tensor(h, h, h, ALU.mult).then_inc(hidden_ready, 1)

            post("post", "post")
            moments("mlp", [D])
            scaled("mlp", xres, xn, 0, KT, col="mlp_pre")
            squares("ff1_1")
            post("mpost", "mlp_post")
            moments("attn2", [D])
            scaled("attn2", xres, xn, 0, KT, col="attn2")

            dve.wait_ge(blk2_loaded, 64)
            dve.wait_ge(pe_done, at("t5_table"))
            tt(t5tab[0:2 * HEADS, :], ps[0:2 * HEADS, 6, :], t5mask[0:2 * HEADS, :], ALU.add, "t5_masked")
            for b in range(2):
                dve.wait_ge(act_done, at("evac", "nk"))
                src = nk[:, b]
                win = bass.AP(src.tensor, src.offset, [list(src.ap[0]), [1, CMP_LEN], [CMP_STRIDE, NCMP]])
                tt(kcp[b], win, cpos[:, b].unsqueeze(2).to_broadcast([P, CMP_LEN, NCMP]), ALU.add, "kcp", b)
            dve.wait_ge(act_done, at("small0"))
            m.did(V.scalar_tensor_tensor(fneg, small0, -1.0, small0, ALU.mult, ALU.max), "f_abs")
            for b, name in enumerate(("cmpk", "cmpv")):
                dve.wait_ge(act_done, at("evac", name))
                tt(ch[:, 2], ch[:, 0], ch[:, 0], ALU.mult)
                m.own()
                ts(ch[:, 2], ch[:, 2], 0.044715, 1.0, ALU.mult, ALU.add)
                m.own()
                tt(ch[:, 1], ch[:, 2], ch[:, 0], ALU.mult, "cmp_in", b)
                dve.wait_ge(act_done, at("cmp_tanh", b))
                m.did(V.scalar_tensor_tensor(ch[:, 3], ch[:, 1], 1.0, ch[:, 0], ALU.add, ALU.mult))
                m.own()
                ts(ch[:, 3], ch[:, 3], 0.5, None, ALU.mult)
                book["cmp_gelu", b] = m.n
            moments("mlan", [384, 128])
            scaled("mlan", mix, mix, 0, 3, 0, "mla_q")
            dve.wait_ge(act_done, at("mlan", "rinv"))
            m.did(V.scalar_tensor_tensor(mix[:, 3], mix[:, 3], gain("mla_kv"), rinv[:, S:2 * S], ALU.mult, ALU.mult), "mlan", "out")
            dve.wait_ge(act_done, at("f_ln"))
            m.did(V.scalar_tensor_tensor(fc8, small0, 0.0, fneg, ALU.min, ALU.subtract))
            m.own()
            m.did(V.tensor_tensor_scan(fneg, ones[:, :], fc8, 0.0, ALU.mult, ALU.add))
            m.own()
            ts(fc8, fneg, HD ** 0.5, None, ALU.mult)
            m.own()
            ts(fneg, fc8, -1.0, None, ALU.mult)
            bc = lambda a, r: a[r].unsqueeze(1).to_broadcast([a[r].shape[0], 4, S])
            r96 = slice(0, 96)
            for b, name in enumerate(("uqar", "uqbr")):
                dve.wait_ge(act_done, at("evac", name))
                q = q96[r96, 4 * b:4 * b + 4]
                tmp = k96[r96, 4 * b:4 * b + 4]
                tt(tmp, tmp, bc(rsin, r96), ALU.mult)
                tt(q, q, bc(rcos, r96), ALU.mult)
                m.own()
                tt(q, q, tmp, ALU.add, "q96", b)
            dve.wait_ge(act_done, at("evac", "small"))
            r32 = slice(64, 96)
            m.own()
            tmp = region[:, 20608:20864]
            dve.wait_ge(act_done, at("evac", "kper"))
            tt(tmp[r32], tmp[r32], rsin[r32], ALU.mult)
            tt(kpe[r32], kpe[r32], rcos[r32], ALU.mult)
            m.own()
            tt(kpe[r32], kpe[r32], tmp[r32], ALU.add)
            m.own()
            m.did(V.tensor_copy(k96[r32, :, :], kpe[r32].unsqueeze(1).to_broadcast([32, 8, S])))
            dve.wait_ge(act_done, at("gates"))
            ts(gates, gates, 1.0, 0.5, ALU.add, ALU.mult)
            ts(rinv[:, S:S + 8], negsink, -1.0, None, ALU.mult)
            dve.wait_ge(t5_loaded, 32)
            m.own()
            m.did(V.memset(st[:, 34:35], 0.0), "ready2")
            negsink = rinv[:, S:S + 8]
            attention("2")
            moments("group", [512] * 4)
            for g in range(4):
                scaled("group", mix, mix, g, 4, 4 * g)
            dve.wait_ge(acc_freed, ACC0["wout2"] + 4)
            tt(xres, xres, xo, ALU.add, "wout2", "added")
            moments("mlp2", [D])
            scaled("mlp2", xres, xn, 0, KT)
            squares("ff1_2")
            dve.wait_ge(acc_freed, ACC0["ff2_2"] + 4)
            tt(xres, xres, xo, ALU.add, "ff2_2", "added")
            moments("final", [D])
            scaled("final", xres, xn, 0, KT)


def pack(inputs):
    a = {k: np.asarray(v) for k, v in inputs.items()}
    f = np.float32
    fm = lambda x: np.ascontiguousarray(x.reshape(S, KT, P).transpose(2, 1, 0))
    cols = lambda v: v.reshape(-1, P).T
    d = {}
    d["xT"], d["memT"] = fm(a["x"][0]), fm(a["mem"][0])
    bf = np.zeros((P, 1), f)
    bf[0:8, 0] = bf[64:72, 0] = a["fox_b_f_2"][0]
    d["gains"] = np.concatenate([
        cols(a["norm_mix_pre"]), cols(a["mem_norm"]), cols(a["out_norm_na"]), cols(a["out_norm_ssm"]), cols(a["out_norm_mem"]),
        cols(a["norm_mix_post"]), cols(a["norm_mlp_pre"]), cols(a["norm_mlp_post"]), cols(a["b_glu"]), cols(a["ssm_d"]),
        cols(a["norm_attn_2"]), cols(a["mla_q_norm_2"]), cols(a["mla_kv_norm_2"]), cols(a["group_norm_2"]),
        cols(a["norm_mlp_2"]), cols(a["final_norm_2"]), bf, np.broadcast_to(a["swa_sinks_2"], (P, HEADS))], 1)
    st = lambda x: x.reshape(2 * GROUPS // 2, P).T
    ldt = np.broadcast_to(a["ssm_log_dt"][0][:, :, None], (2, GROUPS, ST))
    d["ssm_p"] = np.concatenate([st(a["ssm_lam_re"][0]), st(a["ssm_lam_im"][0]), st(ldt)], 1)
    bd, cd = np.zeros((2, 2, 16, 2, ST, 2, CH), f), np.zeros((2, 2, 16, 2, ST, 2, CH), f)
    for i, part in enumerate(("re", "im")):
        b = a["ssm_b_" + part][0].reshape(2, 16, 2, ST, CH)
        c = a["ssm_c_" + part][0].reshape(2, 16, 2, CH, ST).transpose(0, 1, 2, 4, 3)
        for g in range(2):
            bd[i, :, :, g, :, g] = b[:, :, g]
            cd[i, :, :, g, :, g] = c[:, :, g]
    rows = lambda x: np.ascontiguousarray(x.transpose(3, 4, 0, 1, 2, 5, 6).reshape(P, 64, 32))
    d["ssm_b"], d["ssm_c"] = rows(bd), rows(cd)
    for k in ("w_in", "w_mem_kv", "w_glu", "w_out", "w_ff1", "w_ff2", "w_out_2", "w_up_2", "w_down_2"):
        d[k] = a[k][0]
    d["na_rpb"] = np.broadcast_to(a["na_rpb"][0].reshape(1, -1), (GRID_W, NA_HEADS * RPB_H * RPB_W))
    w = a["w_in_2"][0]
    pair = lambda x: x.reshape(D, 2, 4, HD).transpose(0, 2, 1, 3).reshape(D, 512)
    d["w_in_2"] = np.concatenate([
        w[:, 0:512], w[:, 544:1056], w[:, 1056:1568], w[:, 1568:2080], pair(w[:, 2088:2600]),
        w[:, 2600:2856], w[:, 2856:2984], w[:, 3112:3240],
        w[:, 2984:3112], w[:, 3240:3368], w[:, 4032:4160],
        pair(w[:, 3392:3904]), w[:, 3904:4032],
        w[:, 2080:2088], w[:, 3368:3392], w[:, 512:544]], 1)
    w1 = a["nsa_cmp_w1_2"][0].reshape(2, CMP_LEN, HD, HD).transpose(0, 2, 1, 3)
    d["cmp_w1"] = np.concatenate([w1, w1], 1).reshape(2, P, CMP_LEN * HD)
    w2 = np.zeros((2, 64, 2, 2, 64), f)
    for g in range(2):
        w2[g, :, :, g] = a["nsa_cmp_w2_2"][0].transpose(1, 0, 2)
    d["cmp_w2"] = w2.reshape(P, 2 * P)
    pos = a["nsa_cmp_pos_2"][0].transpose(2, 0, 1).reshape(HD, 2 * CMP_LEN)
    d["cmp_pos"] = np.concatenate([pos, pos], 0)
    d["w_uq"] = a["mla_w_uq_2"][0]
    ukv = a["mla_w_ukv_2"][0].reshape(P, HEADS, 2, 64)
    d["w_ukv"] = ukv.transpose(0, 2, 1, 3).reshape(P, 1024)
    d["rel"] = a["rel_bias_2"]
    d.update(constants())
    return {k: np.ascontiguousarray(v) for k, v in d.items()}


def kernel(**inputs):
    import concourse.bacc as bacc
    from concourse.bass_utils import run_bass_kernel_spmd

    data = pack(inputs)

    def build(seen, book):
        nc = bacc.Bacc("TRN2", target_bir_lowering=False, num_devices=1)
        A = {k: nc.dram_tensor(f"in_{k}", v.shape, mybir.dt.from_np(v.dtype), kind="ExternalInput").ap() for k, v in data.items()}
        out = nc.dram_tensor("out", (P, KT, S), mybir.dt.float32, kind="ExternalOutput").ap()
        program(nc, A, out, seen, book)
        return nc

    counts = {}
    build(None, counts)
    nc = build(counts, {})
    r = run_bass_kernel_spmd(nc, [{f"in_{k}": v for k, v in data.items()}], core_ids=[0])
    got = r.results[0]["out"]
    return np.ascontiguousarray(got.transpose(2, 1, 0).reshape(1, S, D))
```

```python
import concourse.bass as bass
from concourse import mybir
from contextlib import ExitStack
import numpy as np

S = 256
P = 128
TT = S // P
D = 2048
KT = D // P
DFF = 4 * D
FT = DFF // P
EPS = 1e-6
NEG = -1e30

GRID_W, WIN_H, WIN_W = 64, 8, 16
RPB_W = 2 * WIN_W - 1
RPB_H = 2 * WIN_H - 1
NA_HEADS, NA_D = 8, 128
MEM_HEADS, MEM_D = 4, 128
GROUPS, CH, ST = 32, 16, 64
SSM_W = 512
CHUNKS = 8
LAM_MAX = -1e-4

HEADS, HD = 8, 64
ROPE = 32
NOPE = 64
CMP_LEN, CMP_STRIDE = 32, 16
NCMP = (S - CMP_LEN) // CMP_STRIDE + 1
BUCKETS, MAX_DIST = 32, 128
SWA_WIN = 128

RING = 4
SPLIT = 2
SLOT = 2048
HALF = SLOT // 2
SK = SLOT // 512

GAINS = [("mix_pre", 16), ("mem", 16), ("out", 16), ("post", 16), ("mlp_pre", 16), ("mlp_post", 16),
         ("b_glu", 4), ("ssm_d", 4), ("attn2", 16), ("mla_q", 3), ("mla_kv", 1), ("group", 16),
         ("mlp2", 16), ("final", 16), ("b_f", 1), ("sinks", 8)]
GCOL = {}
for _n, _w in GAINS:
    GCOL[_n] = sum(w for n, w in GAINS if n in GCOL)
NG = sum(w for _, w in GAINS)

STREAM = [("memk", 4, True, 1), ("memv", 4, True, 1), ("u", 4, False, 1)]
STREAM += [(g, 4, False, 1) for g in ("q0", "q1", "k0", "k1", "v0", "v1", "qm")]
STREAM += [("glu", 1, False, 1), ("wout1", 16, True, 4), ("ff1_1", 64, True, 16), ("ff2_1", 64, True, 4)]
W2_GROUPS = ("mla_c", "fq", "fk", "fv", "nq", "nk", "nv", "sq")
STREAM += [(g, 4, True, 1) for g in W2_GROUPS]
STREAM += [("small", 2, True, 1), ("cmpk", 1, False, 1), ("cmpk2", 0, False, 1), ("cmpv", 1, False, 1), ("cmpv2", 0, False, 1),
           ("uqa", 1, False, 1), ("uqar", 0, False, 1), ("uqb", 1, False, 1), ("uqbr", 0, False, 1), ("kper", 0, False, 1),
           ("kna", 0, False, 1), ("knb", 0, False, 1), ("mv", 1, False, 1),
           ("wout2", 16, True, 4), ("ff1_2", 64, True, 16), ("ff2_2", 64, True, 4)]
SLOT0 = {n: sum(x[1] for x in STREAM[:i]) for i, (n, *_) in enumerate(STREAM)}
SPLIT0 = {n: sum(x[1] for x in STREAM[:i] if x[2]) for i, (n, *_) in enumerate(STREAM)}
ACC0 = {n: sum(x[3] for x in STREAM[:i]) for i, (n, *_) in enumerate(STREAM)}
SPLIT_OF = {}
for _n, _k, _s, _ in STREAM:
    for _j in range(_k if _s else 0):
        SPLIT_OF[SLOT0[_n] + _j] = SPLIT0[_n] + _j


def t5_bucket(d):
    exact = BUCKETS // 2
    d = np.maximum(d, 0)
    large = exact + (np.log(np.maximum(d, 1).astype(np.float32) / np.float32(exact))
                     / np.float32(np.log(MAX_DIST / exact)) * np.float32(BUCKETS - exact)).astype(np.int32)
    return np.where(d < exact, d, np.minimum(large, BUCKETS - 1))


def constants():
    f = np.float32
    c = {}
    c["ident"] = np.eye(P, dtype=f)
    c["iota"] = np.tile(np.arange(S, dtype=f), (P, 1))
    q = np.arange(S)
    cq, cs = q % GRID_W, np.clip(q % GRID_W - WIN_W // 2, 0, GRID_W - WIN_W)
    inside = (cq[None] >= cs[:, None]) & (cq[None] < cs[:, None] + WIN_W)
    tile = lambda m: np.ascontiguousarray(m.reshape(TT, P, -1).transpose(1, 0, 2).reshape(P, -1))
    c["na_mask"] = tile(np.where(inside, 0, NEG).astype(f))
    causal = tile(np.where(q[None] <= q[:, None], 0, NEG).astype(f))
    ends = np.arange(NCMP) * CMP_STRIDE + CMP_LEN - 1
    valid = np.zeros((P, 32), f)
    valid[:, :TT * NCMP] = tile((q[:, None] >= ends[None]).astype(f))
    inv = (f(10000.0) ** (-np.arange(0, ROPE, 2, dtype=f) / f(ROPE))).astype(f)
    ang = q.astype(f)[None] * inv[:, None]
    cos, sin = np.ones((P, S), f), np.zeros((P, S), f)
    cos[NOPE:NOPE + 16] = cos[NOPE + 16:NOPE + 32] = np.cos(ang)
    sin[NOPE:NOPE + 16] = sin[NOPE + 16:NOPE + 32] = np.sin(ang)
    turn = np.zeros((P, NOPE + ROPE), f)
    for j in range(16):
        turn[NOPE + 16 + j, NOPE + j] = -1
        turn[NOPE + j, NOPE + 16 + j] = 1
    c["block2"] = np.concatenate([causal, valid, cos, sin, turn], 1)
    j = np.arange(2 * S)
    dist = S - 1 - j
    hot = np.zeros((P, 2 * S), f)
    hot[t5_bucket(dist), j] = 1
    mask = np.zeros((P, 2 * S), f)
    mask[:2 * HEADS, dist < 0] = NEG
    mask[HEADS:2 * HEADS, dist >= SWA_WIN] = NEG
    c["t5"] = np.concatenate([hot, mask], 1)
    return c


class Marks:

    def __init__(self, eng, sem, book):
        self.eng, self.sem, self.book, self.n = eng, sem, book, 0

    def did(self, ins, *name):
        ins.then_inc(self.sem, 1)
        self.n += 1
        if name:
            self.book[name] = self.n

    def own(self):
        self.eng.wait_ge(self.sem, self.n)


def program(nc, A, out, seen, book):
    f32 = mybir.dt.float32
    ALU = mybir.AluOpType
    ACT = mybir.ActivationFunctionType
    AX = mybir.AxisListType
    ctx = ExitStack()
    with ctx:
        def sem(name):
            return ctx.enter_context(nc.semaphore(name))

        def place(name, a, cols, dt=f32):
            return nc.alloc_sbuf_tensor_at(name, [P, cols], dt, offset=16512 + 4 * a)[:, :]

        def over(name, a, cols):
            return place(name, a, cols, mybir.dt.float32r)

        ring = place("raw_weights", 0, RING * SLOT)
        wh_t, wl_t = over("w_high", 8192, SPLIT * SLOT), over("w_low", 12288, SPLIT * SLOT)
        scratch = place("scratch", 8192, 2 * SPLIT * SLOT)
        xh_t, xl_t = over("x_high", 16384, KT * S), over("x_low", 20480, KT * S)
        xn_t, xl_f = place("x_over_high", 16384, KT * S), place("x_over_low", 20480, KT * S)
        xres_t, mix_t = place("residual", 24576, KT * S), place("mixed", 28672, KT * S)
        mixh_t = over("mem_high", 28672, KT * S)
        region = place("region", 32768, 18784)
        ident, ones, gains = place("ident", 51552, P), place("ones", 51680, S), place("gains", 51936, NG)
        rinv, st = place("rinv", 52120, 4 * S), place("small_stats", 53144, 40)
        ps = ctx.enter_context(nc.psum_tensor("ps", [P, 8, 512], f32))
        t5_dram = nc.dram_tensor("t5_table", (2 * HEADS, P, 2 * S), f32, kind="Internal")

        def tiles(t, a, n, w=S):
            return t[:, a:a + n * w].rearrange("p (t s) -> p t s", s=w)

        xres, xn, mix = tiles(xres_t, 0, KT), tiles(xn_t, 0, KT), tiles(mix_t, 0, KT)
        xh, xl, mixh = tiles(xh_t, 0, KT), tiles(xl_t, 0, KT), tiles(mixh_t, 0, KT)

        def R(a, n, w=S):
            return tiles(region, a, n, w)

        def gain(name, i=0):
            c = GCOL[name] + i
            return gains[:, c:c + 1]

        q1, k1, v1 = R(0, 8), R(2048, 8), R(4096, 2, 1024)
        qm, km, vm, ut = R(6144, 4), R(7168, 4), R(8192, 2, 512), R(9216, 4)
        mem_sq, mem_f, x_sq = R(0, KT), R(4096, KT), R(14592, KT)
        iota = region[:, 10240:10496]
        bbarT, cd, bd = R(10496, 16, P), R(12544, 64, 32), R(8192, 64, 32)
        bt = [R(1024 * i, 32, 32) for i in range(4)]
        cosb = [R(14592, 4), R(15616, 4)]
        sinb = [R(16640, 4), R(17664, 4)]
        gre, gim, t2b, tmpb, ga, gb, gc = (tiles(scratch, 1024 * i, 4) for i in range(7))
        decay, t1b, turns = mix[:, 0:4], mix[:, 4:8], mix[:, 12:16]
        decay_f = mix_t[:, 0:1024]
        na_bias = R(14592, 8, 512)
        na_mask = scratch[:, 7168:7680]
        prob1, probT1 = tiles(scratch, 0, 3, 512), tiles(scratch, 2048, 2, 512)
        ssm = [rinv[:, S + 32 * i:S + 32 * i + 32] for i in range(24)]
        xo, hid_f = R(0, KT), region[:, 0:FT * S]
        spare = R(4096, KT)
        t5 = R(0, 2 * HEADS, 384)
        prob2, probT2 = prob1, probT1
        hot, t5mask, t5tab = (region[:, 17040 + 512 * i:17552 + 512 * i] for i in range(3))
        sq_, sk_ = R(6144, 4), region[:, 7168:7424]
        small0, kpe = region[:, 7424:7680], region[:, 7680:7936]
        nq, nk, nv = R(7936, 4), R(8960, 4), R(9984, 2, 384)
        fq, fk, fv, mv = R(10752, 4), R(11776, 4), R(12800, 2, 512), tiles(xl_f, 0, 2, 512)
        causal = region[:, 13824:14336]
        valid = region[:, 14336:14336 + TT * NCMP].rearrange("p (t c) -> p t c", c=NCMP)
        rcos, rsin = region[:, 14368:14624], region[:, 14624:14880]
        rturn = region[:, 14880:14976]
        kcp = [region[:, 14976 + 480 * i:15456 + 480 * i].rearrange("p (l c) -> p l c", c=NCMP) for i in range(2)]
        kper = region[:, 14976:15232]
        kcmp = region[:, 15936:15936 + NCMP]
        vcmp = region[0:NCMP, 15952:16080]
        ch = region[:, 16080:16144].rearrange("p (a c) -> p a c", c=16)[:, :, 0:NCMP]
        w2bd = region[:, 16144:16400].rearrange("p (a c) -> p a c", c=P)
        fc8, fneg = region[:, 16400:16656], region[:, 16656:16912]
        gates = region[:, 16912:16976].rearrange("p (t c) -> p t c", c=32)
        cpos = region[:, 16976:17040].rearrange("p (a l) -> p a l", l=CMP_LEN)
        q96, k96 = tiles(xn_t, 0, 8), tiles(xn_t, 2048, 8)

        def near(h, keys=slice(0, S)):
            a = t5[:, h]
            n = len(range(S)[keys])
            return bass.AP(a.tensor, a.offset + P + (keys.start or 0), [list(a.ap[0]), [-P, TT], [keys.step or 1, n]])

        def near_tiles(h):
            return [t5[:, h, P * (TT - 1 - t):P * (TT - 1 - t) + P * (t + 1)] for t in range(TT)]

        nmax = st[:, 0:8].rearrange("p (r t) -> p r t", t=2)
        psumr = st[:, 8:16].rearrange("p (r t) -> p r t", t=2)
        pinv = st[:, 16:24].rearrange("p (r t) -> p r t", t=2)
        esink = st[:, 24:32].rearrange("p (r t) -> p r t", t=2)
        halfpi = st[:, 32:33]
        onec = st[:, 33:34]

        pe_done, act_done, dve_done, pool_done = sem("pe_done"), sem("act_done"), sem("dve_done"), sem("pool_done")
        slot_loaded = [sem(f"slot{i}_loaded") for i in range(RING)]
        rounded = sem("rounded")
        split_ready = sem("split_ready")
        split_used = sem("split_used")
        acc_freed = sem("acc_freed")
        hidden_squared = sem("hidden_squared")
        hidden_ready = sem("hidden_ready")
        small_loaded = sem("small_loaded")
        mem_loaded, x_loaded = sem("mem_loaded"), sem("x_loaded")
        ssm_loaded, na_loaded = sem("ssm_loaded"), sem("na_loaded")
        blk2_loaded, t5_in, t5_out, t5_loaded = sem("blk2_loaded"), sem("t5_in"), sem("t5_out"), sem("t5_loaded")
        out_written = sem("out_written")
        block = ctx.enter_context(nc.Block())

        def at(*name):
            return seen[name] if seen is not None else 1

        def accs(name, k=0):
            a = 2 * ((ACC0[name] + k) % 2)
            return ps[:, a:a + 2, :]

        def acc4(name, k=0):
            return accs(name, k).rearrange("p b (h s) -> p (b h) s", s=S)

        def unit(qs, ks, bias, scale, v, mix_tile, base, hd, probs, probTs, nkeys=S, sink=None, gate=None,
                 extra=None, first=True, last=True):
            upto_query = isinstance(bias, list)
            return dict(qs=qs, ks=ks, bias=bias, scale=scale, v=v, mix_tile=mix_tile, base=base, hd=hd, probs=probs,
                        probTs=probTs, n=nkeys, sink=sink, gate=gate, extra=extra, first=first, last=last,
                        keys=[P * (t + 1) if upto_query else nkeys for t in range(TT)])

        causal_tiles = [causal[:, S * t:S * t + P * (t + 1)] for t in range(TT)]
        units = []
        for h in range(MEM_HEADS):
            units.append(unit(qm[:, h], km[:, h], None, MEM_D ** -0.5, lambda kt, h=h: vm[:, kt, P * h:P * h + P],
                              12 + h, 0, P, prob1, probT1))
        for h in range(NA_HEADS):
            units.append(unit(q1[:, h], k1[:, h], na_bias[:, h], NA_D ** -0.5, lambda kt, h=h: v1[:, kt, P * h:P * h + P],
                              h, 0, P, prob1, probT1))
        U1 = len(units)
        half = lambda h: slice(64 * (h % 2), 64 * (h % 2) + 64)
        grp = lambda h: slice(64 * (h // 4), 64 * (h // 4) + 64)
        for h in range(HEADS):
            units.append(unit(sq_[grp(h), h % 4], sk_[grp(h), :], near_tiles(HEADS + h), HD ** -0.5,
                              lambda kt, h=h: nv[:, kt, 256 + 64 * (h // 4):320 + 64 * (h // 4)],
                              12 + h // 2, 64 * (h % 2), HD, prob2, probT2, sink=h))
        for h in range(HEADS):
            for b in range(3):
                if b == 0:
                    cb = near(h, slice(CMP_LEN - 1, S, CMP_STRIDE))
                    units.append(unit(nq[grp(h), h % 4], kcmp[grp(h), :], cb, HD ** -0.5,
                                      lambda kt, h=h: vcmp[:, 64 * (h // 4):64 * (h // 4) + 64],
                                      8 + h // 2, 64 * (h % 2), HD, prob2, probT2, nkeys=NCMP, gate=3 * h,
                                      first=True, last=False))
                else:
                    units.append(unit(nq[grp(h), h % 4], nk[grp(h), 1 + b], near_tiles(h), HD ** -0.5,
                                      lambda kt, h=h, b=b: nv[:, kt, 128 * (b - 1) + 64 * (h // 4):128 * (b - 1) + 64 * (h // 4) + 64],
                                      8 + h // 2, 64 * (h % 2), HD, prob2, probT2, gate=3 * h + b,
                                      first=False, last=b == 2))
        for h in range(HEADS):
            units.append(unit(fq[half(h), h // 2], fk[half(h), h // 2], causal_tiles, HD ** -0.5,
                              lambda kt, h=h: fv[:, kt, 64 * h:64 * h + 64],
                              4 + h // 2, 64 * (h % 2), HD, prob2, probT2, extra=h))
        for h in range(HEADS):
            units.append(unit(q96[0:96, h], k96[0:96, h], causal_tiles, (NOPE + ROPE) ** -0.5,
                              lambda kt, h=h: mv[:, kt, 64 * h:64 * h + 64],
                              h // 2, 64 * (h % 2), HD, prob2, probT2))
        o_of, n_o = [], 0
        for x in units:
            o_of.append(n_o)
            n_o += x["last"]
        RANGE = {"1": (0, U1), "2": (U1, len(units))}

        def scores_ps(i, n):
            return ps[:, 4 + i % 2, 0:TT * n]

        def turned_tiles(x):
            c, r = 0, []
            for kt in range(max(1, x["n"] // P)):
                t0 = next(t for t in range(TT) if x["keys"][t] > P * kt)
                r.append((kt, t0, c))
                c += S - P * t0
            return r

        def out_ps(i):
            x = units[i]
            o = o_of[i] % 2
            return ps[x["base"]:x["base"] + x["hd"], (7, 3)[o], 0:S]

        BODY = 8
        FF1_ITERS = DFF // 1024
        WOUT_ITERS, FF2_ITERS = KT // BODY, FT // BODY

        def ring_slot(n):
            return ring[:, (n % RING) * SLOT:(n % RING + 1) * SLOT]

        def split_slot(t, k):
            return t[:, (k % SPLIT) * SLOT:(k % SPLIT + 1) * SLOT]

        def cut(a, i, off, per, width):
            if isinstance(i, int):
                return a[:, off + i * per:off + i * per + width]
            return a[:, bass.ds(i * per + off, width)]

        @block.sync
        def _(sp):
            state = {"n": 0}

            def load(src, cols=SLOT):
                n = state["n"]
                if n >= RING:
                    if n - RING in SPLIT_OF:
                        sp.wait_ge(split_ready, 2 * (SPLIT_OF[n - RING] + 1))
                    else:
                        sp.wait_ge(pe_done, at("slot", n - RING))
                dst = ring_slot(n)[:, 0:cols]
                if len(src.shape) == 3:
                    dst = dst.rearrange("p (k c) -> p k c", k=src.shape[1])
                sp.dma_start(dst, src).then_inc(slot_loaded[n % RING], 16)
                state["n"] += 1

            def rows(w, c0, width, kt0, n=SK):
                return w[kt0 * P:(kt0 + n) * P, c0:c0 + width].rearrange("(k p) c -> p k c", p=P)

            def group(w, c0, width=512):
                for j in range(KT // SK):
                    load(rows(w, c0, width, SK * j), SK * width)

            def up(name, w):
                for j in range(BODY):
                    load(rows(w, 512 * (j // 4), 512, SK * (j % 4)))
                n0, k0 = SLOT0[name], SPLIT0[name]
                with sp.Fori(1, FF1_ITERS) as i:
                    for j in range(BODY):
                        sp.wait_ge(split_ready, i * (2 * BODY) + 2 * (k0 + j - RING + 1))
                        kt0 = SK * (j % 4)
                        src = w[kt0 * P:(kt0 + SK) * P, bass.ds(i * 1024 + 512 * (j // 4), 512)]
                        sp.dma_start(ring_slot(n0 + j).rearrange("p (k c) -> p k c", k=SK),
                                     src.rearrange("(k p) c -> p k c", p=P)).then_inc(slot_loaded[(n0 + j) % RING], 16)
                state["n"] = n0 + BODY * FF1_ITERS

            def down(name, w, iters):
                for j in range(BODY):
                    load(w[P * j:P * j + P, :])
                n0, k0 = SLOT0[name], SPLIT0[name]
                with sp.Fori(1, iters) as i:
                    for j in range(BODY):
                        sp.wait_ge(split_ready, i * (2 * BODY) + 2 * (k0 + j - RING + 1))
                        sp.dma_start(ring_slot(n0 + j), w[bass.ds(i * (BODY * P) + P * j, P), :]).then_inc(slot_loaded[(n0 + j) % RING], 16)
                state["n"] = n0 + BODY * iters

            group(A["w_mem_kv"], 0)
            group(A["w_mem_kv"], 512)
            w = A["w_in"]
            for c0 in (3072, 0, 512, 1024, 1536, 2048, 2560, 3584):
                group(w, c0)
            load(rows(A["w_glu"], 0, 512, 0))
            down("wout1", A["w_out"], WOUT_ITERS)
            up("ff1_1", A["w_ff1"])
            down("ff2_1", A["w_ff2"], FF2_ITERS)
            w = A["w_in_2"]
            for g in range(6):
                group(w, 512 * g)
            group(w, 3072, 384)
            group(w, 3456, 512)
            for j in range(2):
                load(rows(w, 3968, 256, 8 * j, 8))
            for j in range(2):
                load(A["cmp_w1"][j])
            for j in range(2):
                load(rows(A["w_uq"], 384 * j, 384, 0, 3), 3 * 384)
            load(A["w_ukv"], 1024)
            down("wout2", A["w_out_2"], WOUT_ITERS)
            up("ff1_2", A["w_up_2"])
            down("ff2_2", A["w_down_2"], FF2_ITERS)
            for c in range(4):
                sp.wait_ge(dve_done, at("final", "out", c))
                sp.dma_start(out[:, 4 * c:4 * c + 4], xn[:, 4 * c:4 * c + 4]).then_inc(out_written, 16)
            sp.wait_ge(out_written, 4 * 16)

        chunk_rounded, chunk_ready = sem("chunk_rounded"), sem("chunk_ready")
        CHUNK0 = {"ff2_1": 0, "ff2_2": FT // 4}
        GAINS_OF = {"mlp": "mlp_pre"}

        @block.tensor
        def _(pe):
            m = Marks(pe, pe_done, book)
            state = {"n": 0}

            def take():
                n = state["n"]
                state["n"] += 1
                pe.wait_ge(slot_loaded[n % RING], 16 * (n // RING + 1))
                return n, ring_slot(n)

            def acc_free(name, k=0):
                n = ACC0[name] + k
                if n >= 2:
                    pe.wait_ge(acc_freed, n - 1)

            def wide(acc, w, x, kts, kt, cols=4):
                for c in range(cols):
                    last = nc.tensor.matmul(acc[:, c], w[:, P * c:P * c + P], x, start=(kt == 0 and c % 2 == 0),
                                            stop=(kt == kts - 1), skip_group_check=True)
                return last

            def wide3(acc, wh, wl, xh_, xl_, first, done, cols=4):
                for c in range(cols):
                    o, h = acc[:, c], wh[:, P * c:P * c + P]
                    nc.tensor.matmul(o, h, xh_, start=(first and c % 2 == 0), stop=False, skip_group_check=True)
                    nc.tensor.matmul(o, h, xl_, start=False, stop=False, skip_group_check=True)
                    last = nc.tensor.matmul(o, wl[:, P * c:P * c + P], xh_, start=False, stop=done, skip_group_check=True)
                return last

            def tall(acc, w, x, kts, kt, n=512):
                for t in range(TT):
                    last = nc.tensor.matmul(acc[:, t, 0:n], x[:, P * t:P * t + P], w, start=(kt == 0), stop=(kt == kts - 1))
                return last

            def tall3(acc, wh, wl, xh_, xl_, first, done, n=512):
                for t in range(TT):
                    r = slice(P * t, P * t + P)
                    nc.tensor.matmul(acc[:, t, 0:n], xh_[:, r], wh, start=first, stop=False)
                    nc.tensor.matmul(acc[:, t, 0:n], xh_[:, r], wl, start=False, stop=False)
                    last = nc.tensor.matmul(acc[:, t, 0:n], xl_[:, r], wh, start=False, stop=done)
                return last

            def group(name, x, form="wide", width=512, between=()):
                acc_free(name)
                for j in range(KT // SK):
                    n, w = take()
                    w = w[:, 0:SK * width].rearrange("p (k c) -> p k c", k=SK)
                    for k in range(SK):
                        kt = SK * j + k
                        last = (wide(acc4(name), w[:, k], x[:, kt], KT, kt) if form == "wide"
                                else tall(accs(name), w[:, k], x[:, kt], KT, kt, width))
                    m.did(last, "slot", n)
                    if j == KT // SK - 1:
                        book["acc", name] = m.n
                    for f in between:
                        f(n)

            def group3(name, norm_name, h, l, form="wide", width=512, sk=SK):
                acc_free(name)
                cols = width // P
                for j in range(KT // sk):
                    k = SPLIT_OF[SLOT0[name] + j]
                    for c in range(sk // 4):
                        pe.wait_ge(dve_done, at(norm_name, "out", j * sk // 4 + c))
                    pe.wait_ge(split_ready, 2 * (k + 1))
                    wh, wl = (split_slot(t, k)[:, 0:sk * width].rearrange("p (k c) -> p k c", k=sk) for t in (wh_t, wl_t))
                    for q in range(sk):
                        kt = sk * j + q
                        a = (wh[:, q], wl[:, q], h[:, kt], l[:, kt], kt == 0, kt == KT - 1)
                        last = wide3(acc4(name), *a, cols=cols) if form == "wide" else tall3(accs(name), *a, n=width)
                    last.then_inc(split_used, 1)
                    state["n"] += 1

            def up(name, norm_name):
                k0, a0 = SPLIT0[name], ACC0[name]

                def body(i, first=False):
                    for j in range(BODY):
                        if j == 4 and first:
                            folded_norm(norm_name, spare)
                        k, g = k0 + j, j // 4
                        if j % 4 == 0:
                            pe.wait_ge(acc_freed, i * 2 + (a0 + g - 1))
                        pe.wait_ge(dve_done, at(GAINS_OF.get(norm_name, norm_name), "out", j % 4))
                        pe.wait_ge(split_ready, i * (2 * BODY) + 2 * (k + 1))
                        wh, wl = (split_slot(t, k).rearrange("p (k c) -> p k c", k=SK) for t in (wh_t, wl_t))
                        for q in range(SK):
                            kt = SK * (j % 4) + q
                            last = wide3(acc4(name, g), wh[:, q], wl[:, q], xh[:, kt], xl[:, kt], kt == 0, kt == KT - 1)
                        last.then_inc(split_used, 1)

                body(0, True)
                with pe.Fori(1, FF1_ITERS) as i:
                    body(i)
                state["n"] += BODY * FF1_ITERS

            def down(name, iters, norm_name=None):
                k0, a0 = SPLIT0[name], ACC0[name]
                acc = ps[:, :, :].rearrange("p b (h s) -> p (b h) s", s=S)

                def body(i, first):
                    for j in range(BODY):
                        k = k0 + j
                        if norm_name is None:
                            kt = j
                            if j % 4 == 0:
                                pe.wait_ge(chunk_ready, i * 2 + (CHUNK0[name] + j // 4 + 1))
                        else:
                            kt = BODY * i + j
                            pe.wait_ge(dve_done, at(norm_name, "out", kt // 4))
                        pe.wait_ge(split_ready, i * (2 * BODY) + 2 * (k + 1))
                        last = wide3(acc, split_slot(wh_t, k), split_slot(wl_t, k), xh[:, kt], xl[:, kt],
                                     first and j == 0, True, cols=KT)
                        last.then_inc(split_used, 1)

                pe.wait_ge(acc_freed, a0)
                body(0, True)
                if norm_name is None:
                    with pe.Fori(1, iters) as i:
                        body(i, False)
                else:
                    for i in range(1, iters):
                        body(i, False)
                state["n"] += BODY * iters

            def norm(name, sq, groups):
                for g, (a, n) in enumerate(groups):
                    for t in range(n):
                        if (a + t) % 4 == 0:
                            pe.wait_ge(act_done, at(name, "sq", (a + t) // 4))
                        last = nc.tensor.matmul(ps[:, 4 + g // 2, S * (g % 2):S * (g % 2) + S], ones[:, 0:P], sq[:, a + t],
                                                start=(t == 0), stop=(t == n - 1))
                m.did(last, name, "sum")

            def folded_norm(name, sq):
                pe.wait_ge(dve_done, at(name, "folded"))
                for t in range(4):
                    last = nc.tensor.matmul(ps[:, 4, 0:S], ones[:, 0:P], sq[:, t], start=(t == 0), stop=(t == 3))
                m.did(last, name, "sum")

            def bu(i):
                if i:
                    pe.wait_ge(dve_done, at("yev", i - 1))
                d, jt = i // 4, i % 4
                x = ut[:, jt] if d == 0 else ut[:, jt, ::-1]
                for odd in range(2):
                    for j in (odd, odd + 2):
                        for part in range(2):
                            r = slice(32 * j, 32 * j + 32)
                            last = nc.tensor.matmul(ps[:, 4 + 2 * part + j // 2, S * odd:S * odd + S],
                                                    bbarT[r, 8 * part + i, :], x[r], start=True, stop=True, tile_position=(32 * j, 0))
                    m.did(last, "bu", i)
                    m.own()

            def ssm_y(i):
                pe.wait_ge(dve_done, at("h", i))
                for j in range(4):
                    o = ps[32 * j:32 * j + 32, 4, 0:S]
                    nc.tensor.matmul(o, cd[:, 4 * i + j], t1b[:, j], start=True, stop=False)
                    last = nc.tensor.matmul(o, cd[:, 32 + 4 * i + j], gim[:, j], start=False, stop=True)
                m.did(last, "y", i)

            def attention(which):
                lo, hi = RANGE[which]

                def score(i):
                    x = units[i]
                    n = x["n"]
                    if i - 2 >= lo:
                        pe.wait_ge(dve_done, at("scaled", i - 2))
                    o = scores_ps(i, n)
                    for t in range(TT):
                        w = x["keys"][t]
                        ot = o[:, n * t:n * t + w]
                        ex = x["extra"]
                        last = nc.tensor.matmul(ot, x["qs"][:, P * t:P * t + P], x["ks"][:, 0:w], start=True, stop=ex is None)
                        if ex is not None:
                            b = 64 * (ex % 2)
                            col = ident[b:b + 8, b + ex:b + ex + 1]
                            nc.tensor.matmul(ot, fc8[b:b + 8, P * t:P * t + P], col.to_broadcast([8, w]), start=False, stop=False)
                            last = nc.tensor.matmul(ot, col.to_broadcast([8, P]), fneg[b:b + 8, 0:w], start=False, stop=True)
                    m.did(last, "scores", i)

                def turn(i):
                    x = units[i]
                    n = x["n"]
                    pe.wait_ge(dve_done, at("probs", i))
                    if i - 2 >= lo:
                        pe.wait_ge(act_done, at("probT", i - 2))
                    p = x["probs"][:, i % 3]
                    for kt, t0, c0 in turned_tiles(x):
                        for t in range(t0, TT):
                            w = min(P, n)
                            c = c0 + P * (t - t0)
                            last = nc.tensor.transpose(ps[0:w, (6, 2)[i % 2], c:c + P],
                                                       p[:, n * t + P * kt:n * t + P * kt + w], ident[:, :])
                    m.did(last, "turned", i)

                def value(i):
                    x = units[i]
                    pe.wait_ge(act_done, at("probT", i))
                    if x["first"] and o_of[i] - 2 >= o_of[lo]:
                        pe.wait_ge(act_done, at("out", o_of[i] - 2))
                    nkt = max(1, x["n"] // P)
                    for kt, t0, c0 in turned_tiles(x):
                        last = nc.tensor.matmul(out_ps(i)[:, P * t0:S], x["v"](kt), x["probTs"][0:min(P, x["n"]), i % 2, c0:c0 + S - P * t0],
                                                start=(kt == 0 and x["first"]), stop=(kt == nkt - 1 and x["last"]),
                                                skip_group_check=True)
                    m.did(last, "value", i)

                for i in range(lo, hi + 3):
                    if i < hi:
                        score(i)
                    if lo <= i - 2 < hi:
                        turn(i - 2)
                    if lo <= i - 3:
                        value(i - 3)

            pe.wait_ge(small_loaded, 32)
            pe.wait_ge(dve_done, at("ones"))
            norm("mem", mem_sq, [(0, KT)])
            pe.wait_ge(dve_done, at("mem", "sumread"))
            norm("x", x_sq, [(0, KT)])
            group3("memk", "mem", mixh, xl)
            group3("memv", "mem", mixh, xl, "tall")
            pe.wait_ge(dve_done, at("x", "out"))
            group("u", xn)
            pe.wait_ge(dve_done, at("bbar"))
            pe.wait_ge(dve_done, at("x", "sumread"))
            for part, src in enumerate((bt[2], bt[3])):
                src = src.rearrange("p t s -> p (t s)")
                for k in range(8):
                    o = 8 * part + k
                    last = nc.tensor.transpose(ps[:, 4 + o // 4, P * (o % 4):P * (o % 4) + P], src[:, P * k:P * k + P], ident[:, :])
            m.did(last, "bbar_turned")
            first = state["n"]
            due = {first + (7 * i) // 2: i for i in range(CHUNKS)}

            def ssm_steps(n):
                if n + 1 in due and due[n + 1]:
                    ssm_y(due[n + 1] - 1)
                if n in due:
                    if due[n] == 0:
                        pe.wait_ge(act_done, at("bbarT"))
                        pe.wait_ge(act_done, at("evac", "u"))
                    bu(due[n])

            for g in ("q0", "q1", "k0", "k1"):
                group(g, xn, between=[ssm_steps])
            for g in ("v0", "v1"):
                group(g, xn, "tall", between=[ssm_steps])
            group("qm", xn, between=[ssm_steps])
            ssm_y(CHUNKS - 1)
            pe.wait_ge(dve_done, at("gelu"))
            acc_free("glu")
            n, w = take()
            w = w.rearrange("p (k c) -> p k c", k=SK)
            for k in range(SK):
                last = wide(acc4("glu"), w[:, k], ga[:, k], SK, k)
            m.did(last, "slot", n)
            book["acc", "glu"] = m.n
            pe.wait_ge(act_done, at("evac", "qm"))
            pe.wait_ge(dve_done, at("yev", CHUNKS - 1))
            attention("1")
            norm("outn", xo, [(0, 8), (8, 4), (12, 4)])
            pe.wait_ge(dve_done, at("outn", "sumread"))
            down("wout1", WOUT_ITERS, "outn")
            folded_norm("post", spare)
            up("ff1_1", "mlp")
            down("ff2_1", FF2_ITERS)
            folded_norm("mpost", spare)
            pe.wait_ge(dve_done, at("mpost", "sumread"))
            folded_norm("attn2", mix)

            for g in W2_GROUPS:
                group3(g, "attn2", xh, xl, "tall" if g in ("fv", "nv") else "wide", 384 if g == "nv" else 512)
                if g == "mla_c":
                    pe.wait_ge(t5_in, 32)
                    m.did(nc.tensor.matmul(ps[0:2 * HEADS, 6, :], rinv[0:BUCKETS, S:S + 2 * HEADS], hot[0:BUCKETS, :],
                                           start=True, stop=True), "t5_table")
            group3("small", "attn2", xh, xl, width=256, sk=8)
            for b, name in enumerate(("cmpk", "cmpv")):
                pe.wait_ge(dve_done, at("kcp", b))
                acc_free(name)
                n, w = take()
                w = w.rearrange("p (l c) -> p l c", l=CMP_LEN)
                for g in range(2):
                    r = slice(64 * g, 64 * g + 64)
                    for l in range(CMP_LEN):
                        last = nc.tensor.matmul(accs(name)[r, g, 0:NCMP], w[r, l], kcp[b][r, l], start=(l == 0), stop=(l == CMP_LEN - 1))
                m.did(last, "slot", n)
                book["acc", name] = m.n
                pe.wait_ge(dve_done, at("cmp_gelu", b))
                pe.wait_ge(blk2_loaded, 48)
                acc_free(name + "2")
                if b == 0:
                    m.did(nc.tensor.matmul(accs(name + "2")[:, 0, 0:NCMP], w2bd[:, b], ch[:, 3], start=True, stop=True), "acc", name + "2")
                else:
                    m.did(nc.tensor.matmul(accs(name + "2")[0:NCMP, 0, 0:P], ch[:, 3], w2bd[:, b], start=True, stop=True), "acc", name + "2")
            norm("mlan", mix[:, 4:8], [(0, 3), (3, 1)])
            pe.wait_ge(dve_done, at("mlan", "out"))
            for b, name in enumerate(("uqa", "uqb")):
                acc_free(name)
                n, w = take()
                w = w[:, 0:3 * 384].rearrange("p (k c) -> p k c", k=3)
                for h in range(4):
                    for k in range(3):
                        last = nc.tensor.matmul(acc4(name)[0:96, h], w[:, k, 96 * h:96 * h + 96], mix[:, k], start=(k == 0), stop=(k == 2))
                m.did(last, "slot", n)
                book["acc", name] = m.n
                pe.wait_ge(act_done, at("evac", name))
                acc_free(name + "r")
                for c in range(2):
                    last = nc.tensor.matmul(accs(name + "r")[0:96, c], rturn[0:96, :], q96[0:96, 4 * b + 2 * c:4 * b + 2 * c + 2],
                                            start=True, stop=True)
                m.did(last, "acc", name + "r")
            acc_free("kper")
            pe.wait_ge(act_done, at("evac", "small"))
            m.did(nc.tensor.matmul(accs("kper")[0:96, 0, 0:S], rturn[64:96, :], kpe[64:96, :], start=True, stop=True), "acc", "kper")
            n, w = take()
            for b, name in enumerate(("kna", "knb")):
                acc_free(name)
                for h in range(4):
                    last = nc.tensor.matmul(acc4(name)[0:64, h], w[:, 64 * (4 * b + h):64 * (4 * b + h) + 64], mix[:, 3], start=True, stop=True)
                m.did(last, "acc", name)
            acc_free("mv")
            last = tall(accs("mv"), w[:, 512:1024], mix[:, 3], 1, 0)
            m.did(last, "slot", n)
            book["acc", "mv"] = m.n
            pe.wait_ge(dve_done, at("mlan", "sumread"))
            for t in range(TT):
                last = nc.tensor.transpose(ps[:, 6, 32 * t:32 * t + 32], small0[0:32, P * t:P * t + P], ident[0:32, 0:32])
            m.did(last, "gates_turned")
            pe.wait_ge(act_done, at("gates"))
            pe.wait_ge(dve_done, at("ready2"))
            pe.wait_ge(act_done, at("evac", "mv"))
            attention("2")
            norm("group", xo, [(0, 4), (4, 4), (8, 4), (12, 4)])
            pe.wait_ge(dve_done, at("group", "sumread"))
            down("wout2", WOUT_ITERS, "group")
            up("ff1_2", "mlp2")
            down("ff2_2", FF2_ITERS)
            folded_norm("final", mix)

        @block.scalar
        def _(act):
            m = Marks(act, act_done, book)

            def square(name, src, dst, parts=None, ready=None):
                for c in (range(src.shape[1] // 4) if parts is None else parts):
                    if ready is not None:
                        ready(c)
                    m.did(nc.scalar.activation(dst[:, 4 * c:4 * c + 4], src[:, 4 * c:4 * c + 4], ACT.Square), name, "sq", c)

            def high(name, h, x=mix):
                for c in range(4):
                    act.wait_ge(dve_done, at(name, "full", c))
                    m.did(nc.scalar.activation(h[:, 4 * c:4 * c + 4], x[:, 4 * c:4 * c + 4], ACT.Copy), name, "high", c)

            def high_gained(name, ready):
                for t in range(KT):
                    if t % 4 == 0:
                        ready(t // 4)
                    m.did(nc.scalar.activation(xh[:, t], xres[:, t], ACT.Copy, scale=gain(name, t)), name, "high", t // 4)

            def added(name):
                return lambda c: act.wait_ge(dve_done, at(name, "added", c))

            def summed(name):
                return lambda c: act.wait_ge(acc_freed, ACC0[name] + c + 1)

            def round_slot(name, j, i=0, cols=SLOT):
                n, k = SLOT0[name] + j, SPLIT0[name] + j
                act.wait_ge(slot_loaded[n % RING], i * (16 * BODY // RING) + 16 * (n // RING + 1))
                if k >= SPLIT:
                    act.wait_ge(split_used, i * BODY + (k - SPLIT + 1))
                for h in range(2):
                    r = slice(cols // 2 * h, cols // 2 * (h + 1))
                    nc.scalar.activation(split_slot(wh_t, k)[:, r], ring_slot(n)[:, r], ACT.Copy).then_inc(rounded, 1)

            def root(name, groups):
                act.wait_ge(dve_done, at(name, "rec"))
                r = rinv[:, 0:groups * S]
                m.did(nc.scalar.activation(r, r, ACT.Sqrt), name, "rinv")

            def acc_done(name):
                last = SLOT0[name] + dict((n, k) for n, k, *_ in STREAM)[name] - 1
                if last in SPLIT_OF:
                    act.wait_ge(split_used, SPLIT_OF[last] + 1)
                else:
                    act.wait_ge(pe_done, at("acc", name))

            def evac(name, dst, src=None):
                acc_done(name)
                src = acc4(name) if src is None else src
                nc.scalar.activation(dst, src, ACT.Copy).then_inc(acc_freed, 1)
                act.wait_ge(acc_freed, ACC0[name] + 1)
                m.own()
                m.did(nc.scalar.activation(st[:, 36:37], onec, ACT.Copy), "evac", name)

            def evac_hidden(name, g, i=0):
                act.wait_ge(split_used, i * BODY + (SPLIT0[name] + 4 * (g + 1)))
                act.wait_ge(small_loaded, 32)
                nc.scalar.activation(cut(hid_f, i, 1024 * g, 2048, 1024), accs(name, g).rearrange("p b c -> p (b c)"),
                                     ACT.Relu).then_inc(acc_freed, 1)

            def up(name, norm_name):
                def body(i, first=False):
                    for j in range(2 if first else 0, BODY):
                        round_slot(name, j, i)
                        if first and j in (2, 3):
                            square(norm_name, xres, spare, (2 * j - 4, 2 * j - 3))
                        if j == 0 and not first:
                            evac_hidden(name, -1, i)
                        if j == 4:
                            evac_hidden(name, 0, i)

                body(0, True)
                with act.Fori(1, FF1_ITERS) as i:
                    body(i)

            def chunk(name, q, i=0):
                c = CHUNK0[name] + q
                act.wait_ge(hidden_ready, i * 2 + (c + 1))
                if q >= 2 or not isinstance(i, int):
                    act.wait_ge(split_used, i * BODY + (SPLIT0[name] + 4 * (q - 1)))
                act.wait_ge(small_loaded, 32)
                nc.scalar.activation(xh[:, 4 * (q % 2):4 * (q % 2) + 4].rearrange("p t s -> p (t s)"),
                                     cut(hid_f, i, 1024 * q, 2048, 1024), ACT.Copy).then_inc(chunk_rounded, 1)

            def down(name, iters, pending=None):
                round_slot(name, 0)
                pending()
                chunk(name, 0)
                for j in range(1, BODY):
                    if j == 4:
                        chunk(name, 1)
                    round_slot(name, j)
                with act.Fori(1, iters) as i:
                    for j in range(BODY):
                        if j % 4 == 0:
                            chunk(name, j // 4, i)
                        round_slot(name, j, i)

            def evac_all(name):
                act.wait_ge(split_used, SPLIT0[name] + dict((n, k) for n, k, *_ in STREAM)[name])
                for e in range(4):
                    nc.scalar.activation(region[:, 1024 * e:1024 * e + 1024], ps[:, 2 * e:2 * e + 2, :].rearrange("p b c -> p (b c)"),
                                         ACT.Copy).then_inc(acc_freed, 1)
                act.wait_ge(acc_freed, ACC0[name] + 4)

            def attention(which):
                lo, hi = RANGE[which]

                def exps(i):
                    x = units[i]
                    n = x["n"]
                    act.wait_ge(dve_done, at("max", i))
                    m.own()
                    r = i % 4
                    if x["sink"] is not None:
                        m.did(nc.scalar.activation(esink[:, r], nmax[:, r], ACT.Exp, bias=gain("sinks", x["sink"])))
                    for t in range(TT):
                        s = x["probs"][:, i % 3, n * t:n * t + x["keys"][t]]
                        last = nc.scalar.activation(s, s, ACT.Exp, bias=nmax[:, r, t:t + 1], accum_out=psumr[:, r, t:t + 1])
                        m.did(last, "exp", i)

                def turned(i):
                    x = units[i]
                    act.wait_ge(pe_done, at("turned", i))
                    if i - 2 >= lo:
                        act.wait_ge(pe_done, at("value", i - 2))
                    w = min(P, x["n"])
                    kt, t0, c = turned_tiles(x)[-1]
                    c += S - P * t0
                    m.did(nc.scalar.activation(x["probTs"][0:w, i % 2, 0:c], ps[0:w, (6, 2)[i % 2], 0:c], ACT.Copy), "probT", i)

                def outs(i):
                    x = units[i]
                    if not x["last"]:
                        return
                    act.wait_ge(pe_done, at("value", i))
                    m.did(nc.scalar.activation(mix[x["base"]:x["base"] + x["hd"], x["mix_tile"]], out_ps(i), ACT.Copy), "out", o_of[i])

                for i in range(lo, hi + 4):
                    if lo <= i - 3 < hi:
                        turned(i - 3)
                    if i < hi:
                        exps(i)
                    if lo <= i - 4:
                        outs(i - 4)

            act.dma_start(ident[:, :], A["ident"]).then_inc(small_loaded, 16)
            act.dma_start(gains[:, :], A["gains"]).then_inc(small_loaded, 16)
            act.dma_start(mem_f[:, :, :], A["memT"]).then_inc(mem_loaded, 16)
            act.dma_start(xres[:, :, :], A["xT"]).then_inc(x_loaded, 16)
            act.dma_start(rinv[:, S:S + 96], A["ssm_p"]).then_inc(ssm_loaded, 16)
            act.dma_start(bd, A["ssm_b"]).then_inc(ssm_loaded, 16)
            act.dma_start(cd, A["ssm_c"]).then_inc(ssm_loaded, 16)
            act.dma_start(iota, A["iota"]).then_inc(ssm_loaded, 16)
            act.wait_ge(mem_loaded, 16)
            square("mem", mem_f, mem_sq)
            act.wait_ge(x_loaded, 16)
            square("x", xres, x_sq)
            round_slot("memk", 0)
            round_slot("memk", 1)
            root("mem", 1)
            high("mem", mixh, mem_f)
            root("x", 1)
            act.wait_ge(ssm_loaded, 64)
            dt, mag, s1, c1 = ssm[3], ssm[4], ssm[5], ssm[6]
            m.did(nc.scalar.activation(dt, ssm[2], ACT.Exp), "dt")
            act.wait_ge(dve_done, at("lrdt"))
            m.did(nc.scalar.activation(mag, ssm[7], ACT.Exp), "mag")
            act.wait_ge(dve_done, at("frac"))
            m.did(nc.scalar.activation(s1, ssm[8], ACT.Sin, scale=6.283185))
            m.did(nc.scalar.activation(c1, ssm[9], ACT.Sin, scale=-6.283185, bias=halfpi), "sc1")
            round_slot("memk", 2)
            round_slot("memk", 3)
            round_slot("memv", 0)
            act.wait_ge(dve_done, at("mem", "out", 3))
            evac("memk", km)
            for j in range(1, 4):
                round_slot("memv", j)
            act.wait_ge(dve_done, at("bbar"))
            evac("memv", vm, accs("memv"))
            evac("u", ut)
            act.wait_ge(pe_done, at("bbar_turned"))
            m.did(nc.scalar.activation(bbarT.rearrange("p a s -> p (a s)"), ps[:, 4:8, :].rearrange("p b c -> p (b c)"), ACT.Copy), "bbarT")

            def tables(i):
                act.wait_ge(pool_done, at("turns", i))
                if i >= 2:
                    act.wait_ge(dve_done, at("h", i - 2))
                else:
                    act.wait_ge(dve_done, at("bbar"))
                m.did(nc.scalar.activation(sinb[i % 2], turns, ACT.Sin, scale=6.283185))
                m.own()
                m.did(nc.scalar.activation(turns, turns, ACT.Abs))
                m.own()
                m.did(nc.scalar.activation(cosb[i % 2], turns, ACT.Sin, scale=-6.283185, bias=halfpi), "tables", i)

            tables(0)
            tables(1)
            for c, (name, dst, src) in enumerate([("q0", q1[:, 0:4], None), ("q1", q1[:, 4:8], None), ("k0", k1[:, 0:4], None), ("k1", k1[:, 4:8], None),
                                    ("v0", v1[:, :, 0:512], accs("v0")), ("v1", v1[:, :, 512:1024], accs("v1")),
                                    ("qm", qm, None)]):
                if c + 2 < CHUNKS:
                    tables(c + 2)
                evac(name, dst, src)
            act.wait_ge(dve_done, at("gelu_in"))
            m.did(nc.scalar.activation(gb, gb, ACT.Tanh, scale=0.7978845608028654), "gelu_tanh")
            act.wait_ge(pe_done, at("acc", "glu"))
            act.wait_ge(dve_done, at("half_b"))
            for c in range(4):
                last = nc.scalar.activation(gb[:, c], acc4("glu")[:, c], ACT.Tanh, scale=0.5, bias=gc[:, c, 0:1])
                if c < 3:
                    m.did(last)
                else:
                    last.then_inc(acc_freed, 1)
            act.wait_ge(acc_freed, ACC0["glu"] + 1)
            m.own()
            m.did(nc.scalar.activation(st[:, 36:37], onec, ACT.Copy), "glu_gate")
            act.wait_ge(dve_done, at("h", CHUNKS - 1))
            act.wait_ge(pe_done, at("y", CHUNKS - 1))
            act.dma_start(na_mask, A["na_mask"]).then_inc(na_loaded, 16)
            rpb = A["na_rpb"]
            for r in range(S // GRID_W):
                for rk in range(S // GRID_W):
                    src = bass.AP(rpb.tensor, (rk - r + WIN_H - 1) * RPB_W + WIN_W - 1, [[NA_HEADS * RPB_H * RPB_W - 1, GRID_W], [RPB_H * RPB_W, NA_HEADS], [1, GRID_W]])
                    c0 = S * (r // 2) + GRID_W * rk
                    act.dma_start(na_bias[64 * (r % 2):64 * (r % 2) + 64, :, c0:c0 + GRID_W], src).then_inc(na_loaded, 16)
            attention("1")
            m.own()
            act.wait_ge(dve_done, at("ssm_out"))
            act.wait_ge(pe_done, at("value", U1 - 1))
            square("outn", mix, xo)
            round_slot("wout1", 0)
            round_slot("wout1", 1)
            root("outn", 3)
            high("outn", xh)
            for j in range(2, 2 * BODY):
                round_slot("wout1", j)
            evac_all("wout1")
            square("post", xo, spare, (2, 3))
            round_slot("ff1_1", 0)
            round_slot("ff1_1", 1)
            root("post", 1)
            high_gained("mlp_pre", added("post"))
            up("ff1_1", "mlp")
            down("ff2_1", FF2_ITERS, lambda: evac_hidden("ff1_1", 1, FF1_ITERS - 1))
            evac_all("ff2_1")
            square("mpost", xo, spare, (2, 3))
            round_slot("mla_c", 0)
            round_slot("mla_c", 1)
            root("mpost", 1)
            square("attn2", xres, mix, ready=added("mpost"))
            root("attn2", 1)
            high("attn2", xh)

            act.dma_start(hot, A["t5"][:, 0:512]).then_inc(t5_in, 16)
            act.dma_start(rinv[0:BUCKETS, S:S + 2 * HEADS], A["rel"]).then_inc(t5_in, 16)
            act.dma_start(t5mask, A["t5"][:, 512:1024]).then_inc(blk2_loaded, 16)
            act.dma_start(region[:, 13824:14976], A["block2"]).then_inc(blk2_loaded, 16)
            act.dma_start(region[:, 16144:16400], A["cmp_w2"]).then_inc(blk2_loaded, 16)
            act.dma_start(region[:, 16976:17040], A["cmp_pos"]).then_inc(blk2_loaded, 16)
            round_slot("mla_c", 2)
            round_slot("mla_c", 3)
            round_slot("fq", 0)
            act.wait_ge(dve_done, at("attn2", "out", 3))
            evac("mla_c", mix[:, 0:4])
            act.wait_ge(dve_done, at("t5_masked"))
            act.dma_start(t5_dram.ap(), t5tab[0:2 * HEADS, :].unsqueeze(1).to_broadcast([2 * HEADS, P, 2 * S])).then_inc(t5_out, 16)
            act.wait_ge(t5_out, 16)
            src = bass.AP(t5_dram.ap().tensor, P - 1, [[2 * S - 1, P], [2 * S * P, 2 * HEADS], [1, 384]])
            act.dma_start(t5, src).then_inc(t5_loaded, 16)
            m.own()
            square("mlan", mix[:, 0:4], mix[:, 4:8])
            chain = [("fq", fq, None), ("fk", fk, None), ("fv", fv, accs("fv")), ("nq", nq, None), ("nk", nk, None),
                     ("nv", nv, accs("nv")[:, :, 0:384]), ("sq", sq_, None)]
            for c, (name, dst, src) in enumerate(chain):
                for j in range(1, 4):
                    round_slot(name, j, cols=SK * 384 if name == "nv" else SLOT)
                nxt = chain[c + 1][0] if c + 1 < len(chain) else "small"
                round_slot(nxt, 0, cols=SK * 384 if nxt == "nv" else SLOT)
                evac(name, dst, src)
            round_slot("small", 1)
            acc_done("small")
            m.did(nc.scalar.activation(sk_, acc4("small")[:, 0], ACT.Copy))
            m.did(nc.scalar.activation(small0, acc4("small")[:, 1], ACT.Identity, bias=gain("b_f")), "small0")
            nc.scalar.activation(kpe[64:96, :], acc4("small")[96:128, 1], ACT.Copy).then_inc(acc_freed, 1)
            act.wait_ge(acc_freed, ACC0["small"] + 1)
            m.own()
            m.did(nc.scalar.activation(st[:, 36:37], onec, ACT.Copy), "evac", "small")
            for b, name in enumerate(("cmpk", "cmpv")):
                act.wait_ge(pe_done, at("acc", name))
                if b:
                    act.wait_ge(pe_done, at("acc", "cmpk2"))
                m.did(nc.scalar.activation(ch[0:64, 0], accs(name)[0:64, 0, 0:NCMP], ACT.Copy))
                nc.scalar.activation(ch[64:128, 0], accs(name)[64:128, 1, 0:NCMP], ACT.Copy).then_inc(acc_freed, 1)
                act.wait_ge(acc_freed, ACC0[name] + 1)
                m.own()
                m.did(nc.scalar.activation(st[:, 36:37], onec, ACT.Copy), "evac", name)
                act.wait_ge(dve_done, at("cmp_in", b))
                m.did(nc.scalar.activation(ch[:, 1], ch[:, 1], ACT.Tanh, scale=0.7978845608028654), "cmp_tanh", b)
                if b == 0:
                    evac("cmpk2", kcmp, accs("cmpk2")[:, 0, 0:NCMP])
                else:
                    evac("cmpv2", vcmp, accs("cmpv2")[0:NCMP, 0, 0:P])
            root("mlan", 2)
            act.wait_ge(dve_done, at("f_abs"))
            m.did(nc.scalar.activation(fneg, fneg, ACT.Exp, scale=-1.0))
            m.own()
            m.did(nc.scalar.activation(fneg, fneg, ACT.Ln, bias=onec), "f_ln")
            for b, name in enumerate(("uqa", "uqb")):
                evac(name, q96[0:96, 4 * b:4 * b + 4], acc4(name)[0:96])
                evac(name + "r", k96[0:96, 4 * b:4 * b + 4], acc4(name + "r")[0:96])
            act.wait_ge(dve_done, at("kcp", 1))
            act.wait_ge(pe_done, at("acc", "cmpv"))
            evac("kper", kper[64:96], accs("kper")[64:96, 0, 0:S])
            for b, name in enumerate(("kna", "knb")):
                act.wait_ge(dve_done, at("q96", b))
                evac(name, k96[0:64, 4 * b:4 * b + 4], acc4(name)[0:64])
            evac("mv", mv, accs("mv"))
            act.wait_ge(pe_done, at("gates_turned"))
            m.did(nc.scalar.activation(gates, ps[:, 6, 0:64].rearrange("p (t c) -> p t c", c=32), ACT.Tanh, scale=0.5), "gates")
            act.wait_ge(dve_done, at("ready2"))
            attention("2")
            m.own()
            act.wait_ge(pe_done, at("value", len(units) - 1))
            square("group", mix, xo)
            round_slot("wout2", 0)
            round_slot("wout2", 1)
            root("group", 4)
            high("group", xh)
            for j in range(2, 2 * BODY):
                round_slot("wout2", j)
            high_gained("mlp2", summed("wout2"))
            round_slot("ff1_2", 0)
            round_slot("ff1_2", 1)
            up("ff1_2", "mlp2")
            down("ff2_2", FF2_ITERS, lambda: evac_hidden("ff1_2", 1, FF1_ITERS - 1))
            square("final", xres, mix, ready=summed("ff2_2"))
            root("final", 1)

        @block.gpsimd
        def _(pool):
            m = Marks(pool, pool_done, book)
            MAGIC = 12582912.0
            pool.wait_ge(dve_done, at("frac"))
            pool.wait_ge(ssm_loaded, 64)
            pool.wait_ge(split_used, SPLIT0["memv"] + 4)
            pool.wait_ge(dve_done, at("bbar"))
            time = iota.unsqueeze(1).to_broadcast([P, 4, S])
            for i in range(CHUNKS):
                col = lambda k: ssm[k][:, 4 * i:4 * i + 4].unsqueeze(2).to_broadcast([P, 4, S])
                if i:
                    pool.wait_ge(act_done, at("tables", i - 1))
                m.did(nc.gpsimd.tensor_tensor(tmpb, time, col(8), ALU.mult))
                m.own()
                m.did(nc.gpsimd.tensor_scalar(tmpb, tmpb, MAGIC, MAGIC, ALU.add, ALU.subtract))
                m.did(nc.gpsimd.tensor_tensor(turns, time, col(10), ALU.mult))
                m.own()
                m.did(nc.gpsimd.tensor_tensor(turns, turns, tmpb, ALU.subtract))
                m.own()
                m.did(nc.gpsimd.tensor_tensor(tmpb, time, col(11), ALU.mult))
                m.own()
                m.did(nc.gpsimd.tensor_tensor(turns, turns, tmpb, ALU.add))
                m.own()
                m.did(nc.gpsimd.tensor_scalar(turns, turns, 0.5, -0.5, ALU.min, ALU.max), "turns", i)

        @block.vector
        def _(dve):
            m = Marks(dve, dve_done, book)
            V = nc.vector

            def tt(o, a, b, op, *name):
                m.did(V.tensor_tensor(o, a, b, op), *name)

            def fold(name, sq, product=None):
                for c in range(2 if product is not None else 0):
                    dve.wait_ge(acc_freed, ACC0[product] + c + 1)
                    r = slice(4 * c, 4 * c + 4)
                    tt(sq[:, r], xo[:, r], xo[:, r], ALU.mult)
                for c in range(1, 4):
                    if product is None or c > 1:
                        dve.wait_ge(act_done, at(name, "sq", c))
                    m.own()
                    tt(sq[:, 0:4], sq[:, 0:4], sq[:, 4 * c:4 * c + 4], ALU.add, name, "folded")

            def moments(name, dims, at_col=0):
                dve.wait_ge(pe_done, at(name, "sum"))
                m.own()
                for g, d in enumerate(dims):
                    last = V.tensor_scalar(rinv[:, at_col + S * g:at_col + S * g + S], ps[:, 4 + g // 2, S * (g % 2):S * (g % 2) + S],
                                           1.0 / d, EPS, ALU.mult, ALU.add)
                    m.did(last, name, "sumread")
                m.own()
                r = rinv[:, at_col:at_col + len(dims) * S]
                m.did(V.reciprocal(r, r), name, "rec")

            def low_gained(name, c):
                dve.wait_ge(act_done, at(name, "high", c))
                for t in range(4 * c, 4 * c + 4):
                    m.did(V.scalar_tensor_tensor(xl[:, t], xres[:, t], gain(name, t), xh[:, t].bitcast(f32),
                                                 ALU.mult, ALU.subtract), name, "out", c)

            def add_product(name):
                n = dict((n, k) for n, k, *_ in STREAM)[name]
                dve.wait_ge(split_used, SPLIT0[name] + n)
                for c in range(4):
                    r = slice(4 * c, 4 * c + 4)
                    src = ps[:, 2 * c:2 * c + 2, :].rearrange("p b (h s) -> p (b h) s", s=S)
                    V.tensor_tensor(xres[:, r], xres[:, r], src, ALU.add).then_inc(acc_freed, 1)
                dve.wait_ge(acc_freed, ACC0[name] + 4)

            def low(name, j, i=0, cols=SLOT):
                n, k = SLOT0[name] + j, SPLIT0[name] + j
                for h in range(2):
                    dve.wait_ge(rounded, i * (2 * BODY) + (2 * k + h + 1))
                    r = slice(cols // 2 * h, cols // 2 * (h + 1))
                    V.tensor_tensor(split_slot(wl_t, k)[:, r], ring_slot(n)[:, r], split_slot(wh_t, k)[:, r].bitcast(f32),
                                    ALU.subtract).then_inc(split_ready, 1)

            def norm_split(name, src, full, h, l, groups, col=None):
                dve.wait_ge(act_done, at(name, "rinv"))
                m.own()

                def lows(c):
                    dve.wait_ge(act_done, at(name, "high", c))
                    r = slice(4 * c, 4 * c + 4)
                    tt(l[:, r], full[:, r], h[:, r].bitcast(f32), ALU.subtract, name, "out", c)

                for c in range(4):
                    for t in range(4 * c, 4 * c + 4):
                        g = [g for g, (a, n) in enumerate(groups) if a <= t < a + n][0]
                        m.did(V.scalar_tensor_tensor(full[:, t], src[:, t], gain(col or name, t), rinv[:, S * g:S * g + S],
                                                     ALU.mult, ALU.mult), name, "full", c)
                    if c:
                        lows(c - 1)
                lows(3)

            def up(name, norm_name):
                factor = rinv[:, S:2 * S].unsqueeze(1).to_broadcast([P, 4, S])
                g0 = 0 if name == "ff1_1" else DFF // 512

                def squared(g, i):
                    h = cut(hid_f, i, 1024 * g, 2048, 1024)
                    h4 = h.rearrange("p (t s) -> p t s", s=S)
                    dve.wait_ge(acc_freed, i * 2 + (ACC0[name] + g + 1))
                    V.tensor_tensor(h, h, h, ALU.mult).then_inc(hidden_squared, 1)
                    dve.wait_ge(hidden_squared, i * 2 + (g0 + g + 1))
                    V.tensor_tensor(h4, h4, factor, ALU.mult).then_inc(hidden_ready, 1)

                def body(i, first=False):
                    for j in range(2 if first else 0, BODY):
                        low(name, j, i)
                        if j == 1 and not first:
                            squared(-1, i)
                        if j == 3 and first:
                            fold(norm_name, spare)
                        if j == 5:
                            if first:
                                moments(norm_name, [D], S)
                                m.own()
                            squared(0, i)

                body(0, True)
                with dve.Fori(1, FF1_ITERS) as i:
                    body(i)
                return lambda: squared(1, FF1_ITERS - 1)

            def down(name, pending):
                def chunk(q, i=0):
                    r = slice(4 * (q % 2), 4 * (q % 2) + 4)
                    dve.wait_ge(chunk_rounded, i * 2 + (CHUNK0[name] + q + 1))
                    fl = lambda a: a.rearrange("p t s -> p (t s)")
                    V.tensor_tensor(fl(xl[:, r]), cut(hid_f, i, 1024 * q, 2048, 1024), fl(xh[:, r]).bitcast(f32),
                                    ALU.subtract).then_inc(chunk_ready, 1)

                low(name, 0)
                pending()
                chunk(0)
                for j in range(1, BODY):
                    if j == 4:
                        chunk(1)
                    low(name, j)
                with dve.Fori(1, FF2_ITERS) as i:
                    for j in range(BODY):
                        if j % 4 == 0:
                            chunk(j // 4, i)
                        low(name, j, i)

            def scaled(name, src, dst, g, n, a=0, col=None):
                dve.wait_ge(act_done, at(name, "rinv"))
                m.own()
                for t in range(n):
                    m.did(V.scalar_tensor_tensor(dst[:, a + t], src[:, a + t], gain(col or name, a + t), rinv[:, S * g:S * g + S],
                                                 ALU.mult, ALU.mult), name, "out")
                    if t % 4 == 3:
                        book[name, "out", t // 4] = m.n

            def attention(which, between=()):
                lo, hi = RANGE[which]

                def scale(i):
                    x = units[i]
                    n, r = x["n"], i % 4
                    dve.wait_ge(pe_done, at("scores", i))
                    if i - 3 >= lo:
                        dve.wait_ge(pe_done, at("turned", i - 3))
                    if i - 4 >= lo:
                        dve.wait_ge(act_done, at("exp", i - 4))
                    m.own()
                    s = x["probs"][:, i % 3, 0:TT * n]
                    k3 = lambda a: a.rearrange("p (t k) -> p t k", k=n)
                    if x["bias"] is None:
                        ins = V.tensor_scalar(s, scores_ps(i, n), x["scale"], None, ALU.mult)
                    elif isinstance(x["bias"], list):
                        for t, w in enumerate(x["keys"]):
                            r_ = slice(n * t, n * t + w)
                            ins = V.scalar_tensor_tensor(s[:, r_], scores_ps(i, n)[:, r_], x["scale"], x["bias"][t], ALU.mult, ALU.add)
                            if t == 0:
                                m.did(ins)
                    elif len(x["bias"].shape) == 2:
                        ins = V.scalar_tensor_tensor(s, scores_ps(i, n), x["scale"], x["bias"], ALU.mult, ALU.add)
                    else:
                        ins = V.scalar_tensor_tensor(k3(s), k3(scores_ps(i, n)), x["scale"], x["bias"], ALU.mult, ALU.add)
                    m.did(ins, "scaled", i)
                    m.own()
                    if isinstance(x["bias"], list):
                        for t, w in enumerate(x["keys"]):
                            m.did(V.tensor_reduce(nmax[:, r, t:t + 1], s[:, n * t:n * t + w], AX.X, ALU.max, negate=True), "max", i)
                    else:
                        m.did(V.tensor_reduce(nmax[:, r], k3(s), AX.X, ALU.max, negate=True), "max", i)
                    if x["sink"] is not None:
                        m.own()
                        m.did(V.tensor_scalar(nmax[:, r], nmax[:, r], negsink[:, x["sink"]:x["sink"] + 1], None, ALU.min), "max", i)

                def normal(i):
                    x = units[i]
                    n, r = x["n"], i % 4
                    dve.wait_ge(act_done, at("exp", i))
                    if x["sink"] is not None:
                        tt(psumr[:, r], psumr[:, r], esink[:, r], ALU.add)
                        m.own()
                    m.did(V.reciprocal(pinv[:, r], psumr[:, r]))
                    m.own()
                    if x["gate"] is not None:
                        tt(pinv[:, r], pinv[:, r], gates[:, :, 8 + x["gate"]], ALU.mult)
                        m.own()
                    for t in range(TT):
                        s = x["probs"][:, i % 3, n * t:n * t + x["keys"][t]]
                        if n == S:
                            ins = V.tensor_scalar(s, s, pinv[:, r, t:t + 1], None, ALU.mult)
                        else:
                            ins = V.scalar_tensor_tensor(s, s, pinv[:, r, t:t + 1], valid[:, t], ALU.mult, ALU.mult)
                        m.did(ins, "probs", i)

                for i in range(lo, hi + 1):
                    if i < hi:
                        scale(i)
                    if lo <= i - 1:
                        normal(i - 1)
                    for f in between:
                        f(i)

            V.memset(ones[:, :], 1.0)
            V.memset(halfpi, float(np.float32(np.pi / 2)))
            m.did(V.memset(onec, 1.0), "ones")
            dve.wait_ge(small_loaded, 32)
            low("memk", 0)
            low("memk", 1)
            moments("mem", [D])
            norm_split("mem", mem_f, mem_f, mixh, xl, [(0, KT)])
            moments("x", [D])
            scaled("x", xres, xn, 0, KT, col="mix_pre")
            dve.wait_ge(ssm_loaded, 64)
            dve.wait_ge(act_done, at("dt"))
            lr, li, dt, mag, s1, c1 = ssm[0], ssm[1], ssm[3], ssm[4], ssm[5], ssm[6]
            lrdt, f, af, fhi, flo, th, nn, a1, a2, a3, wr, wi = ssm[7:19]
            MAGIC = 12582912.0
            ts = lambda o, a, x, y, p, q=None: m.did(V.tensor_scalar(o, a, x, y, p, q) if q is not None else V.tensor_scalar(o, a, x, None, p))
            ts(lr, lr, LAM_MAX, None, ALU.min)
            m.own()
            tt(lrdt, lr, dt, ALU.mult, "lrdt")
            tt(th, li, dt, ALU.mult)
            m.own()
            ts(nn, th, float(np.float32(1 / (2 * np.pi))), MAGIC, ALU.mult, ALU.add)
            m.own()
            ts(nn, nn, MAGIC, None, ALU.subtract)
            m.own()
            c_hi = 6.28125
            c_mid = float(np.float32(2 * np.pi - c_hi))
            c_lo = float(np.float32(2 * np.pi - c_hi - c_mid))
            for c in (c_hi, c_mid, c_lo):
                m.did(V.scalar_tensor_tensor(th, nn, -c, th, ALU.mult, ALU.add))
                m.own()
            ts(f, th, float(np.float32(1 / (2 * np.pi))), None, ALU.mult)
            m.own()
            ts(f, f, 0.5, -0.5, ALU.min, ALU.max)
            m.own()
            m.did(V.scalar_tensor_tensor(af, f, -1.0, f, ALU.mult, ALU.max))
            ts(fhi, f, 192.0, 192.0, ALU.add, ALU.subtract)
            m.own()
            tt(flo, f, fhi, ALU.subtract, "frac")
            dve.wait_ge(act_done, at("sc1"))
            tt(a1, mag, c1, ALU.mult)
            tt(a2, mag, s1, ALU.mult)
            m.own()
            ts(a1, a1, -1.0, None, ALU.add)
            tt(nn, lr, lr, ALU.mult)
            tt(th, li, li, ALU.mult)
            m.own()
            tt(nn, nn, th, ALU.add)
            m.own()
            m.did(V.reciprocal(nn, nn))
            tt(wr, a1, lr, ALU.mult)
            tt(th, a2, li, ALU.mult)
            tt(wi, a2, lr, ALU.mult)
            tt(a3, a1, li, ALU.mult)
            m.own()
            tt(wr, wr, th, ALU.add)
            tt(wi, wi, a3, ALU.subtract)
            m.own()
            tt(wr, wr, nn, ALU.mult)
            tt(wi, wi, nn, ALU.mult)
            m.own()
            wide32 = lambda a: a.unsqueeze(2).to_broadcast([P, 32, 32])
            bre, bim = bd[:, 0:32], bd[:, 32:64]
            x1, x2, br, bi = bt
            tt(br, bre, wide32(wr), ALU.mult)
            tt(x1, bim, wide32(wi), ALU.mult)
            tt(bi, bim, wide32(wr), ALU.mult)
            tt(x2, bre, wide32(wi), ALU.mult)
            m.own()
            tt(br, br, x1, ALU.subtract)
            tt(bi, bi, x2, ALU.add, "bbar")
            ts(cd[:, 32:64], cd[:, 32:64], -1.0, None, ALU.mult)
            low("memk", 2)
            low("memk", 3)
            for j in range(4):
                low("memv", j)
            dve.wait_ge(split_used, SPLIT0["memv"] + 4)

            def decays(i):
                m.did(V.tensor_copy(decay, mag[:, 4 * i:4 * i + 4].unsqueeze(2).to_broadcast([P, 4, S])))
                m.own()
                m.did(V.memset(decay[:, :, 0:1], 0.0))

            flat = lambda a: a.rearrange("p t s -> p (t s)")
            decays(0)
            for i in range(CHUNKS):
                cs, sn = cosb[i % 2], sinb[i % 2]
                bur = ps[:, 4:6, :].rearrange("p b (h s) -> p (b h) s", s=S)
                bui = ps[:, 6:8, :].rearrange("p b (h s) -> p (b h) s", s=S)
                dve.wait_ge(pe_done, at("bu", i))
                m.own()
                dve.wait_ge(act_done, at("tables", i))
                if i == 0:
                    dve.wait_ge(act_done, at("bbarT"))
                tt(t1b, bur, cs, ALU.mult)
                tt(t2b, bui, sn, ALU.mult)
                m.own()
                tt(gre, t1b, t2b, ALU.add)
                m.own()
                tt(t1b, bui, cs, ALU.mult)
                tt(t2b, bur, sn, ALU.mult)
                m.own()
                tt(gim, t1b, t2b, ALU.subtract)
                m.own()
                for g in (gre, gim):
                    m.did(V.tensor_tensor_scan(flat(g), decay_f, flat(g), 0.0, ALU.mult, ALU.add))
                m.own()
                tt(t1b, cs, gre, ALU.mult)
                tt(t2b, sn, gim, ALU.mult)
                m.own()
                tt(t1b, t1b, t2b, ALU.subtract)
                m.own()
                tt(t2b, sn, gre, ALU.mult)
                m.own()
                tt(gim, cs, gim, ALU.mult)
                m.own()
                tt(gim, t2b, gim, ALU.add, "h", i)
                if i + 1 < CHUNKS:
                    decays(i + 1)
                d, jt = i // 4, i % 4
                dve.wait_ge(pe_done, at("y", i))
                m.own()
                yp = ps[:, 4, 0:S]
                o = mix[:, 8 + jt]
                if d == 0:
                    m.did(V.scalar_tensor_tensor(o, ut[:, jt], gain("ssm_d", jt), yp, ALU.mult, ALU.add), "yev", i)
                else:
                    tt(o, yp[:, ::-1], o, ALU.add, "yev", i)
            y = mix[:, 8:12]
            m.own()
            tt(ga, y, y, ALU.mult)
            m.own()
            ts(ga, ga, 0.044715, 1.0, ALU.mult, ALU.add)
            m.own()
            tt(gb, ga, y, ALU.mult, "gelu_in")
            dve.wait_ge(act_done, at("gelu_tanh"))
            m.did(V.scalar_tensor_tensor(ga, gb, 1.0, y, ALU.add, ALU.mult))
            m.own()
            ts(ga, ga, 0.5, None, ALU.mult)
            book["gelu",] = m.n
            ts(gc[:, :, 0:1], gains[:, GCOL["b_glu"]:GCOL["b_glu"] + 4].unsqueeze(2), 0.5, None, ALU.mult)
            book["half_b",] = m.n
            dve.wait_ge(act_done, at("glu_gate"))
            m.did(V.scalar_tensor_tensor(gb, gb, 1.0, ga, ALU.add, ALU.mult))
            m.own()
            ts(y, gb, 0.5, None, ALU.mult)
            book["ssm_out",] = m.n
            negsink = gains[:, GCOL["sinks"]:GCOL["sinks"] + 8]

            def add_mask(i):
                if i == MEM_HEADS - 1:
                    dve.wait_ge(na_loaded, 16 * 17)
                    m.did(V.tensor_tensor(na_bias, na_bias, na_mask.unsqueeze(1).to_broadcast([P, 8, 512]), ALU.add))
                    m.own()

            attention("1", [add_mask])
            low("wout1", 0)
            low("wout1", 1)
            moments("outn", [1024, 512, 512])
            norm_split("outn", mix, mix, xh, xl, [(0, 8), (8, 4), (12, 4)], "out")
            for j in range(2, 2 * BODY):
                low("wout1", j)

            def post(name, product, col, first, then=None):
                fold(name, spare, product)
                low(first, 0)
                low(first, 1)
                moments(name, [D])
                for c in range(4):
                    scaled(name, xo, xo, 0, 4, 4 * c, col)
                    m.own()
                    r = slice(4 * c, 4 * c + 4)
                    tt(xres[:, r], xres[:, r], xo[:, r], ALU.add, name, "added", c)
                    if then is not None and c:
                        then(c - 1)
                if then is not None:
                    then(3)

            post("post", "wout1", "post", "ff1_1", lambda c: low_gained("mlp_pre", c))
            down("ff2_1", up("ff1_1", "mlp"))
            post("mpost", "ff2_1", "mlp_post", "mla_c")
            fold("attn2", mix)
            moments("attn2", [D])
            norm_split("attn2", xres, mix, xh, xl, [(0, KT)])
            low("mla_c", 2)
            low("mla_c", 3)
            low("fq", 0)

            dve.wait_ge(blk2_loaded, 64)
            dve.wait_ge(pe_done, at("t5_table"))
            tt(t5tab[0:2 * HEADS, :], ps[0:2 * HEADS, 6, :], t5mask[0:2 * HEADS, :], ALU.add, "t5_masked")
            for c, name in enumerate(W2_GROUPS[1:]):
                width = lambda g: SK * 384 if g == "nv" else SLOT
                for j in range(1, 4):
                    low(name, j, cols=width(name))
                nxt = W2_GROUPS[c + 2] if c + 2 < len(W2_GROUPS) else "small"
                low(nxt, 0, cols=width(nxt))
            low("small", 1)
            for b in range(2):
                dve.wait_ge(act_done, at("evac", "nk"))
                src = nk[:, b]
                win = bass.AP(src.tensor, src.offset, [list(src.ap[0]), [1, CMP_LEN], [CMP_STRIDE, NCMP]])
                tt(kcp[b], win, cpos[:, b].unsqueeze(2).to_broadcast([P, CMP_LEN, NCMP]), ALU.add, "kcp", b)
            dve.wait_ge(act_done, at("small0"))
            m.did(V.scalar_tensor_tensor(fneg, small0, -1.0, small0, ALU.mult, ALU.max), "f_abs")
            for b, name in enumerate(("cmpk", "cmpv")):
                dve.wait_ge(act_done, at("evac", name))
                tt(ch[:, 2], ch[:, 0], ch[:, 0], ALU.mult)
                m.own()
                ts(ch[:, 2], ch[:, 2], 0.044715, 1.0, ALU.mult, ALU.add)
                m.own()
                tt(ch[:, 1], ch[:, 2], ch[:, 0], ALU.mult, "cmp_in", b)
                dve.wait_ge(act_done, at("cmp_tanh", b))
                m.did(V.scalar_tensor_tensor(ch[:, 3], ch[:, 1], 1.0, ch[:, 0], ALU.add, ALU.mult))
                m.own()
                ts(ch[:, 3], ch[:, 3], 0.5, None, ALU.mult)
                book["cmp_gelu", b] = m.n
            moments("mlan", [384, 128])
            scaled("mlan", mix, mix, 0, 3, 0, "mla_q")
            dve.wait_ge(act_done, at("mlan", "rinv"))
            m.did(V.scalar_tensor_tensor(mix[:, 3], mix[:, 3], gain("mla_kv"), rinv[:, S:2 * S], ALU.mult, ALU.mult), "mlan", "out")
            dve.wait_ge(act_done, at("f_ln"))
            m.did(V.scalar_tensor_tensor(fc8, small0, 0.0, fneg, ALU.min, ALU.subtract))
            m.own()
            m.did(V.tensor_tensor_scan(fneg, ones[:, :], fc8, 0.0, ALU.mult, ALU.add))
            m.own()
            ts(fc8, fneg, HD ** 0.5, None, ALU.mult)
            m.own()
            ts(fneg, fc8, -1.0, None, ALU.mult)
            bc = lambda a, r: a[r].unsqueeze(1).to_broadcast([a[r].shape[0], 4, S])
            r96 = slice(0, 96)
            for b, name in enumerate(("uqar", "uqbr")):
                dve.wait_ge(act_done, at("evac", name))
                q = q96[r96, 4 * b:4 * b + 4]
                tmp = k96[r96, 4 * b:4 * b + 4]
                tt(tmp, tmp, bc(rsin, r96), ALU.mult)
                tt(q, q, bc(rcos, r96), ALU.mult)
                m.own()
                tt(q, q, tmp, ALU.add, "q96", b)
            dve.wait_ge(act_done, at("evac", "small"))
            r32 = slice(64, 96)
            m.own()
            tmp = kper
            dve.wait_ge(act_done, at("evac", "kper"))
            tt(tmp[r32], tmp[r32], rsin[r32], ALU.mult)
            tt(kpe[r32], kpe[r32], rcos[r32], ALU.mult)
            m.own()
            tt(kpe[r32], kpe[r32], tmp[r32], ALU.add)
            m.own()
            m.did(V.tensor_copy(k96[r32, :, :], kpe[r32].unsqueeze(1).to_broadcast([32, 8, S])))
            dve.wait_ge(act_done, at("gates"))
            ts(gates, gates, 1.0, 0.5, ALU.add, ALU.mult)
            ts(rinv[:, S:S + 8], negsink, -1.0, None, ALU.mult)
            dve.wait_ge(t5_loaded, 16)
            m.own()
            m.did(V.memset(st[:, 34:35], 0.0), "ready2")
            negsink = rinv[:, S:S + 8]
            attention("2")
            low("wout2", 0)
            low("wout2", 1)
            moments("group", [512] * 4)
            norm_split("group", mix, mix, xh, xl, [(0, 4), (4, 4), (8, 4), (12, 4)])
            for j in range(2, 2 * BODY):
                low("wout2", j)
            add_product("wout2")
            for c in range(4):
                low_gained("mlp2", c)
            low("ff1_2", 0)
            low("ff1_2", 1)
            down("ff2_2", up("ff1_2", "mlp2"))
            add_product("ff2_2")
            fold("final", mix)
            moments("final", [D])
            scaled("final", xres, xn, 0, KT)


def pack(inputs):
    a = {k: np.asarray(v) for k, v in inputs.items()}
    f = np.float32
    fm = lambda x: np.ascontiguousarray(x.reshape(S, KT, P).transpose(2, 1, 0))
    cols = lambda v: v.reshape(-1, P).T
    d = {}
    d["xT"], d["memT"] = fm(a["x"][0]), fm(a["mem"][0])
    bf = np.zeros((P, 1), f)
    bf[0:8, 0] = bf[64:72, 0] = a["fox_b_f_2"][0]
    d["gains"] = np.concatenate([
        cols(a["norm_mix_pre"]), cols(a["mem_norm"]), cols(a["out_norm_na"]), cols(a["out_norm_ssm"]), cols(a["out_norm_mem"]),
        cols(a["norm_mix_post"]), cols(a["norm_mlp_pre"]), cols(a["norm_mlp_post"]), cols(a["b_glu"]), cols(a["ssm_d"]),
        cols(a["norm_attn_2"]), cols(a["mla_q_norm_2"]), cols(a["mla_kv_norm_2"]), cols(a["group_norm_2"]),
        cols(a["norm_mlp_2"]), cols(a["final_norm_2"]), bf, np.broadcast_to(a["swa_sinks_2"], (P, HEADS))], 1)
    st = lambda x: x.reshape(2 * GROUPS // 2, P).T
    ldt = np.broadcast_to(a["ssm_log_dt"][0][:, :, None], (2, GROUPS, ST))
    d["ssm_p"] = np.concatenate([st(a["ssm_lam_re"][0]), st(a["ssm_lam_im"][0]), st(ldt)], 1)
    bd, cd = np.zeros((2, 2, 16, 2, ST, 2, CH), f), np.zeros((2, 2, 16, 2, ST, 2, CH), f)
    for i, part in enumerate(("re", "im")):
        b = a["ssm_b_" + part][0].reshape(2, 16, 2, ST, CH)
        c = a["ssm_c_" + part][0].reshape(2, 16, 2, CH, ST).transpose(0, 1, 2, 4, 3)
        for g in range(2):
            bd[i, :, :, g, :, g] = b[:, :, g]
            cd[i, :, :, g, :, g] = c[:, :, g]
    rows = lambda x: np.ascontiguousarray(x.transpose(3, 4, 0, 1, 2, 5, 6).reshape(P, 64, 32))
    d["ssm_b"], d["ssm_c"] = rows(bd), rows(cd)
    for k in ("w_in", "w_mem_kv", "w_glu", "w_out", "w_ff1", "w_ff2", "w_out_2", "w_up_2", "w_down_2"):
        d[k] = a[k][0]
    d["na_rpb"] = np.broadcast_to(a["na_rpb"][0].reshape(1, -1), (GRID_W, NA_HEADS * RPB_H * RPB_W))
    w = a["w_in_2"][0]
    pair = lambda x: x.reshape(D, 2, 4, HD).transpose(0, 2, 1, 3).reshape(D, 512)
    d["w_in_2"] = np.concatenate([
        w[:, 0:512], w[:, 544:1056], w[:, 1056:1568], w[:, 1568:2080], pair(w[:, 2088:2600]),
        w[:, 2600:2856], w[:, 2856:2984], w[:, 3112:3240],
        w[:, 2984:3112], w[:, 3240:3368], w[:, 4032:4160],
        pair(w[:, 3392:3904]), w[:, 3904:4032],
        *(2 * [w[:, 2080:2088], w[:, 3368:3392], w[:, 512:544]])], 1)
    w1 = a["nsa_cmp_w1_2"][0].reshape(2, CMP_LEN, HD, HD).transpose(0, 2, 1, 3)
    d["cmp_w1"] = np.concatenate([w1, w1], 1).reshape(2, P, CMP_LEN * HD)
    w2 = np.zeros((2, 64, 2, 2, 64), f)
    for g in range(2):
        w2[g, :, :, g] = a["nsa_cmp_w2_2"][0].transpose(1, 0, 2)
    d["cmp_w2"] = w2.reshape(P, 2 * P)
    pos = a["nsa_cmp_pos_2"][0].transpose(2, 0, 1).reshape(HD, 2 * CMP_LEN)
    d["cmp_pos"] = np.concatenate([pos, pos], 0)
    d["w_uq"] = a["mla_w_uq_2"][0]
    ukv = a["mla_w_ukv_2"][0].reshape(P, HEADS, 2, 64)
    d["w_ukv"] = ukv.transpose(0, 2, 1, 3).reshape(P, 1024)
    d["rel"] = a["rel_bias_2"]
    d.update(constants())
    return {k: np.ascontiguousarray(v) for k, v in d.items()}


def kernel(**inputs):
    import concourse.bacc as bacc
    from concourse.bass_utils import run_bass_kernel_spmd

    data = pack(inputs)

    def build(seen, book):
        nc = bacc.Bacc("TRN2", target_bir_lowering=False, num_devices=1)
        A = {k: nc.dram_tensor(f"in_{k}", v.shape, mybir.dt.from_np(v.dtype), kind="ExternalInput").ap() for k, v in data.items()}
        out = nc.dram_tensor("out", (P, KT, S), mybir.dt.float32, kind="ExternalOutput").ap()
        program(nc, A, out, seen, book)
        return nc

    counts = {}
    build(None, counts)
    nc = build(counts, {})
    r = run_bass_kernel_spmd(nc, [{f"in_{k}": v for k, v in data.items()}], core_ids=[0])
    got = r.results[0]["out"]
    return np.ascontiguousarray(got.transpose(2, 1, 0).reshape(1, S, D))
```
